# Optimizing a Trainium2 kernel written in Bass

```python
import math
import jax, jax.numpy as jnp
from jax import lax
import numpy as np

D_MODEL = 2048
BATCH = 1
SEQ = 256
DEPTH = 2
DEC_BATCH = 1
DEC_SEQ = 64
PAST_LEN = 128

CHUNK = 64
D_MIX = D_MODEL
A_HEADS = 4
A_HEAD_DIM = 128
A_WIDTH = A_HEADS * A_HEAD_DIM
IDX_HEADS = 16
IDX_DIM = 64
DSA_TOPK = 256
B_HEADS = 4
B_HEAD_DIM = 128
B_WIDTH = B_HEADS * B_HEAD_DIM
B_PREV_CHUNKS = 8
B_WIN = B_PREV_CHUNKS * CHUNK
REL_CLIP = 128
C_WIDTH = D_MIX - A_WIDTH - B_WIDTH
C_HEAD_DIM = 64
C_HEADS = C_WIDTH // C_HEAD_DIM
C_GROUPS = 4
C_STATE = 128
CONV_W = 4
CONV_DIM = C_WIDTH + 2 * C_GROUPS * C_STATE
D_FF = 4 * D_MODEL
ROPE_THETA = 500000.0
EPS = 1e-5

_COLS = (A_WIDTH, A_WIDTH, A_WIDTH, IDX_HEADS * IDX_DIM, IDX_DIM, IDX_HEADS,
         B_WIDTH, B_WIDTH, B_WIDTH,
         C_WIDTH, CONV_DIM, C_HEADS)
SPLIT_OFFSETS = tuple(int(v) for v in np.cumsum(_COLS)[:-1])
IN_COLS = int(sum(_COLS))

kernel_name = "hybrid_stream_dsa_band_ssd_step"

def rms_norm(x, w):
    x32 = x.astype(jnp.float32)
    y = x32 * lax.rsqrt(jnp.mean(x32 * x32, axis=-1, keepdims=True) + EPS)
    return y.astype(x.dtype) * w

def partial_rope(x, pos):
    d = x.shape[-1]
    rot = d // 4
    half = rot // 2
    inv = ROPE_THETA ** (-jnp.arange(half, dtype=jnp.float32) * 2.0 / rot)
    ang = pos.astype(jnp.float32)[:, None] * inv[None, :]
    cos = jnp.cos(ang)[None, :, None, :]
    sin = jnp.sin(ang)[None, :, None, :]
    x32 = x.astype(jnp.float32)
    x1, x2 = x32[..., :half], x32[..., half:rot]
    out = jnp.concatenate([x1 * cos - x2 * sin, x2 * cos + x1 * sin, x32[..., rot:]], axis=-1)
    return out.astype(x.dtype)

def dsa_select_attend(q, qi, wi, k, v, ki, limit, topk):
    S = k.shape[1]
    d = q.shape[-1]
    idx_logits = jnp.einsum('bqhd,bsd->bqhs', qi, ki).astype(jnp.float32) * IDX_DIM ** -0.5
    score = jnp.einsum('bqhs,bqh->bqs', jax.nn.relu(idx_logits), wi.astype(jnp.float32))
    admissible = jnp.arange(S) < limit
    score = jnp.where(admissible[None, None, :], score, -jnp.inf)
    _, sel = lax.top_k(score, topk)
    valid = sel < limit
    kg = jax.vmap(lambda kk, ii: kk[ii])(k, sel)
    vg = jax.vmap(lambda vv, ii: vv[ii])(v, sel)
    logits = jnp.einsum('bqhd,bqkhd->bhqk', q, kg).astype(jnp.float32) * d ** -0.5
    logits = jnp.where(valid[:, None, :, :], logits, -jnp.inf)
    p = jax.nn.softmax(logits, axis=-1).astype(v.dtype)
    return jnp.einsum('bhqk,bqkhd->bqhd', p, vg)

def dsa_prompt(q, qi, wi, k, v, ki):
    b, t = q.shape[:2]
    nc = t // CHUNK
    topk = min(DSA_TOPK, t // 4)

    def one_chunk(c):
        s0 = c * CHUNK
        sl = lambda a: lax.dynamic_slice_in_dim(a, s0, CHUNK, axis=1)
        return dsa_select_attend(sl(q), sl(qi), sl(wi), k, v, ki, s0 + CHUNK, topk)

    o = lax.map(one_chunk, jnp.arange(nc))
    return jnp.moveaxis(o, 0, 1).reshape(b, t, A_HEADS, A_HEAD_DIM)

def dsa_sample(q, qi, wi, k, v, ki):
    L = k.shape[1]
    topk = min(DSA_TOPK, L // 4)

    def one_seq(a):
        return dsa_select_attend(*[z[None] for z in a], L, topk)[0]

    return lax.map(one_seq, (q, qi, wi, k, v, ki))

def rel_bias(table, rel):
    return table[:, jnp.clip(rel, -REL_CLIP, REL_CLIP) + REL_CLIP]

def band_attn_prompt(q, k, v, table):
    b, t, h, d = q.shape
    nc = t // CHUNK
    nb = B_PREV_CHUNKS + 1
    qc = q.reshape(b, nc, CHUNK, h, d)
    pad = ((0, 0), (B_WIN, 0), (0, 0), (0, 0))
    kc = jnp.pad(k, pad).reshape(b, nc + B_PREV_CHUNKS, CHUNK, h, d)
    vc = jnp.pad(v, pad).reshape(b, nc + B_PREV_CHUNKS, CHUNK, h, d)
    band_idx = jnp.arange(nc)[:, None] + jnp.arange(nb)[None, :]
    kb = kc[:, band_idx].reshape(b, nc, nb * CHUNK, h, d)
    vb = vc[:, band_idx].reshape(b, nc, nb * CHUNK, h, d)
    j = jnp.arange(nb * CHUNK)
    rel = (B_WIN + jnp.arange(CHUNK))[:, None] - j[None, :]
    valid = (jnp.arange(nc)[:, None] * CHUNK - B_WIN + j[None, :]) >= 0
    logits = jnp.einsum('bcqhd,bckhd->bchqk', qc, kb).astype(jnp.float32) * d ** -0.5
    logits = logits + rel_bias(table, rel).astype(jnp.float32)[None, None]
    logits = jnp.where(valid[None, :, None, None, :], logits, -jnp.inf)
    p = jax.nn.softmax(logits, axis=-1).astype(v.dtype)
    o = jnp.einsum('bchqk,bckhd->bcqhd', p, vb)
    return o.reshape(b, t, h, d)

def band_attn_sample(q, k_new, v_new, k_buf, v_buf, table):
    t = q.shape[1]
    d = q.shape[-1]
    nbuf = k_buf.shape[1]
    k = jnp.concatenate([k_buf, k_new], axis=1)
    v = jnp.concatenate([v_buf, v_new], axis=1)
    rel = (nbuf + jnp.arange(t))[:, None] - jnp.arange(nbuf + t)[None, :]
    logits = jnp.einsum('bqhd,bkhd->bhqk', q, k).astype(jnp.float32) * d ** -0.5
    logits = logits + rel_bias(table, rel).astype(jnp.float32)[None]
    p = jax.nn.softmax(logits, axis=-1).astype(v.dtype)
    return jnp.einsum('bhqk,bkhd->bqhd', p, v)

def causal_dwconv(x, buf, w, bias):
    t = x.shape[1]
    xp = jnp.concatenate([buf, x], axis=1)
    y = bias + xp[:, 0:t] * w[0]
    for j in range(1, CONV_W):
        y = y + xp[:, j:j + t] * w[j]
    return y, xp[:, -(CONV_W - 1):]

def segsum(a):
    T = a.shape[-1]
    cs = jnp.cumsum(a, axis=-1)
    seg = cs[..., :, None] - cs[..., None, :]
    mask = jnp.tril(jnp.ones((T, T), dtype=bool))
    return jnp.where(mask, seg, -jnp.inf)

def ssd_scan(x, dt, a, bm, cm, h0, block):
    b, L, H, P = x.shape
    nc = L // block
    xd = (x * dt[..., None]).reshape(b, nc, block, H, P)
    ad = (dt * a).reshape(b, nc, block, H).transpose(0, 3, 1, 2)
    bm = bm.reshape(b, nc, block, H, -1)
    cm = cm.reshape(b, nc, block, H, -1)
    a_cs = jnp.cumsum(ad, axis=-1)
    decay_in = jnp.exp(segsum(ad))
    cb = jnp.einsum('bclhn,bcshn->bhcls', cm, bm)
    y_diag = jnp.einsum('bhcls,bcshp->bclhp', cb * decay_in, xd)
    decay_to_end = jnp.exp(a_cs[..., -1:] - a_cs)
    chunk_states = jnp.einsum('bclhn,bhcl,bclhp->bchpn', bm, decay_to_end, xd)
    states = jnp.concatenate([h0[:, None], chunk_states], axis=1)
    chunk_decay = jnp.exp(segsum(jnp.pad(a_cs[..., -1], ((0, 0), (0, 0), (1, 0)))))
    states = jnp.einsum('bhzc,bchpn->bzhpn', chunk_decay, states)
    h_in, h_last = states[:, :-1], states[:, -1]
    y_off = jnp.einsum('bclhn,bchpn,bhcl->bclhp', cm, h_in, jnp.exp(a_cs))
    return (y_diag + y_off).reshape(b, L, H, P), h_last

def ssd_mixer(z, xbc, dt_raw, conv_buf, h0, conv_w, conv_b, dt_bias, a_log, d_skip, gate_norm, block):
    f32 = jnp.float32
    b, t = z.shape[:2]
    xbc_c, new_buf = causal_dwconv(xbc, conv_buf, conv_w, conv_b)
    xbc_c = jax.nn.silu(xbc_c)
    xs, bs, cs = jnp.split(xbc_c, [C_WIDTH, C_WIDTH + C_GROUPS * C_STATE], axis=-1)
    rep = C_HEADS // C_GROUPS
    xs = xs.reshape(b, t, C_HEADS, C_HEAD_DIM).astype(f32)
    bs = jnp.repeat(bs.reshape(b, t, C_GROUPS, C_STATE).astype(f32), rep, axis=2)
    cs = jnp.repeat(cs.reshape(b, t, C_GROUPS, C_STATE).astype(f32), rep, axis=2)
    dt = jax.nn.softplus(dt_raw.astype(f32) + dt_bias.astype(f32))
    a = -jnp.exp(a_log.astype(f32))
    y, h_last = ssd_scan(xs, dt, a, bs, cs, h0.astype(f32), block)
    y = (y + d_skip.astype(f32)[:, None] * xs).reshape(b, t, C_WIDTH)
    g = (y * jax.nn.silu(z.astype(f32))).reshape(b, t, C_GROUPS, C_WIDTH // C_GROUPS)
    g = g * lax.rsqrt(jnp.mean(g * g, axis=-1, keepdims=True) + EPS)
    out = g.reshape(b, t, C_WIDTH).astype(z.dtype) * gate_norm
    return out, h_last.astype(z.dtype), new_buf

def trunk_layer(x, pos, lw, past):
    (norm1, w_in, w_out, b_rel, conv_w, conv_b, dt_bias, a_log, d_skip, gate_norm,
     norm2, w_up, w_down) = lw
    b, t, _ = x.shape
    h = rms_norm(x, norm1)
    proj = jnp.einsum('btd,de->bte', h, w_in)
    aq, ak, av, iq, ik, iw, bq, bk, bv, cz, cxbc, cdt = jnp.split(proj, SPLIT_OFFSETS, axis=-1)
    aq = partial_rope(aq.reshape(b, t, A_HEADS, A_HEAD_DIM), pos)
    ak = partial_rope(ak.reshape(b, t, A_HEADS, A_HEAD_DIM), pos)
    av = av.reshape(b, t, A_HEADS, A_HEAD_DIM)
    iq = partial_rope(iq.reshape(b, t, IDX_HEADS, IDX_DIM), pos)
    ik = partial_rope(ik.reshape(b, t, 1, IDX_DIM), pos)[:, :, 0]
    iw = iw * IDX_HEADS ** -0.5
    bq = bq.reshape(b, t, B_HEADS, B_HEAD_DIM)
    bk = bk.reshape(b, t, B_HEADS, B_HEAD_DIM)
    bv = bv.reshape(b, t, B_HEADS, B_HEAD_DIM)
    if past is None:
        o_a = dsa_prompt(aq, iq, iw, ak, av, ik)
        o_b = band_attn_prompt(bq, bk, bv, b_rel)
        conv_buf = jnp.zeros((b, CONV_W - 1, CONV_DIM), x.dtype)
        h0 = jnp.zeros((b, C_HEADS, C_HEAD_DIM, C_STATE), jnp.float32)
        block = CHUNK
        nkeep = min(B_WIN, t)
        b_k_rows, b_v_rows = bk[:, t - nkeep:], bv[:, t - nkeep:]
    else:
        pk, pv, pki, pbk, pbv, ph, pconv = past
        o_a = dsa_sample(aq, iq, iw,
                         jnp.concatenate([pk, ak], axis=1),
                         jnp.concatenate([pv, av], axis=1),
                         jnp.concatenate([pki, ik], axis=1))
        o_b = band_attn_sample(bq, bk, bv, pbk, pbv, b_rel)
        conv_buf, h0, block = pconv, ph, t
        b_k_rows, b_v_rows = bk, bv
    o_c, h_last, conv_new = ssd_mixer(cz, cxbc, cdt, conv_buf, h0, conv_w, conv_b,
                                      dt_bias, a_log, d_skip, gate_norm, block)
    mix = jnp.concatenate([o_a.reshape(b, t, A_WIDTH), o_b.reshape(b, t, B_WIDTH), o_c], axis=-1)
    x = x + jnp.einsum('bte,ed->btd', mix, w_out)
    u = jax.nn.relu(jnp.einsum('btd,df->btf', rms_norm(x, norm2), w_up))
    x = x + jnp.einsum('btf,fd->btd', jnp.square(u), w_down)
    return x, (ak, av, ik, b_k_rows, b_v_rows, h_last, conv_new)

def stack_states(states):
    return [jnp.stack([s[i] for s in states], axis=0) for i in range(7)]

def setup_inputs(seed: int = 0) -> dict:
    key = jax.random.key(seed)
    ks = jax.random.split(key, 24)
    f32 = jnp.float32

    def nrm(k, shape, s):
        return jax.random.normal(k, shape, f32) * s

    b_cache = min(B_WIN, PAST_LEN)
    dt0 = jnp.exp(jax.random.uniform(ks[15], (DEPTH, C_HEADS), f32, math.log(1e-3), math.log(1e-1)))
    return {
        "x_prompt": nrm(ks[0], (BATCH, SEQ, D_MODEL), 1.0),
        "x_sample": nrm(ks[1], (DEC_BATCH, DEC_SEQ, D_MODEL), 1.0),
        "cache_a_k": nrm(ks[2], (DEPTH, DEC_BATCH, PAST_LEN, A_HEADS, A_HEAD_DIM), 1.0),
        "cache_a_v": nrm(ks[3], (DEPTH, DEC_BATCH, PAST_LEN, A_HEADS, A_HEAD_DIM), 1.0),
        "cache_a_kidx": nrm(ks[4], (DEPTH, DEC_BATCH, PAST_LEN, IDX_DIM), 1.0),
        "cache_b_k": nrm(ks[5], (DEPTH, DEC_BATCH, b_cache, B_HEADS, B_HEAD_DIM), 1.0),
        "cache_b_v": nrm(ks[6], (DEPTH, DEC_BATCH, b_cache, B_HEADS, B_HEAD_DIM), 1.0),
        "state_ssm": nrm(ks[7], (DEPTH, DEC_BATCH, C_HEADS, C_HEAD_DIM, C_STATE), 0.5),
        "state_conv": nrm(ks[8], (DEPTH, DEC_BATCH, CONV_W - 1, CONV_DIM), 1.0),
        "norm1": 1.0 + nrm(ks[9], (DEPTH, D_MODEL), 0.02),
        "w_in": nrm(ks[10], (DEPTH, D_MODEL, IN_COLS), D_MODEL ** -0.5),
        "w_out": nrm(ks[11], (DEPTH, D_MIX, D_MODEL), 0.5 * D_MIX ** -0.5),
        "b_rel": nrm(ks[12], (DEPTH, B_HEADS, 2 * REL_CLIP + 1), 0.1),
        "conv_w": nrm(ks[13], (DEPTH, CONV_W, CONV_DIM), CONV_W ** -0.5),
        "conv_b": nrm(ks[14], (DEPTH, CONV_DIM), 0.01),
        "dt_bias": dt0 + jnp.log(-jnp.expm1(-dt0)),
        "a_log": jnp.log(jax.random.uniform(ks[16], (DEPTH, C_HEADS), f32, 1.0, 16.0)),
        "d_skip": 1.0 + nrm(ks[17], (DEPTH, C_HEADS), 0.1),
        "gate_norm": 1.0 + nrm(ks[18], (DEPTH, C_WIDTH), 0.02),
        "norm2": 1.0 + nrm(ks[19], (DEPTH, D_MODEL), 0.02),
        "w_up": nrm(ks[20], (DEPTH, D_MODEL, D_FF), D_MODEL ** -0.5),
        "w_down": nrm(ks[21], (DEPTH, D_FF, D_MODEL), 0.5 * D_FF ** -0.5),
        "final_norm": 1.0 + nrm(ks[22], (D_MODEL,), 0.02),
    }

def reference(x_prompt, x_sample, cache_a_k, cache_a_v, cache_a_kidx, cache_b_k, cache_b_v,
              state_ssm, state_conv, norm1, w_in, w_out, b_rel, conv_w, conv_b, dt_bias,
              a_log, d_skip, gate_norm, norm2, w_up, w_down, final_norm):
    past_len = cache_a_k.shape[2]
    pos_p = jnp.arange(x_prompt.shape[1])
    pos_s = past_len + jnp.arange(x_sample.shape[1])
    xp, xs = x_prompt, x_sample
    new_p, new_s = [], []
    for l in range(DEPTH):
        lw = (norm1[l], w_in[l], w_out[l], b_rel[l], conv_w[l], conv_b[l], dt_bias[l], a_log[l],
              d_skip[l], gate_norm[l], norm2[l], w_up[l], w_down[l])
        xp, st_p = trunk_layer(xp, pos_p, lw, None)
        past = (cache_a_k[l], cache_a_v[l], cache_a_kidx[l], cache_b_k[l], cache_b_v[l],
                state_ssm[l], state_conv[l])
        xs, st_s = trunk_layer(xs, pos_s, lw, past)
        new_p.append(st_p)
        new_s.append(st_s)
    y_prompt = rms_norm(xp, final_norm)
    y_sample = rms_norm(xs, final_norm)
    p_a_k, p_a_v, p_a_kidx, p_b_k, p_b_v, p_ssm, p_conv = stack_states(new_p)
    s_a_k, s_a_v, s_a_kidx, s_b_k, s_b_v, s_ssm, s_conv = stack_states(new_s)
    return (y_prompt, y_sample, p_a_k, p_a_v, p_a_kidx, p_b_k, p_b_v, p_ssm, p_conv,
            s_a_k, s_a_v, s_a_kidx, s_b_k, s_b_v, s_ssm, s_conv)


_drawn_inputs = setup_inputs


def setup_inputs(seed=0):
    import zlib

    import numpy as np

    out = dict(_drawn_inputs(seed))
    spreads = {}
    factors = {'b_rel': 26.571,
     'conv_b': 3.052,
     'gate_norm': 5.425,
     'norm2': 3.311,
     'final_norm': 22.331,
     'cache_b_k': 3.921,
     'cache_b_v': 3.051,
     'cache_a_k': 2.731}
    for name, (base, spread) in spreads.items():
        noise = np.random.default_rng([zlib.crc32(name.encode()), seed]).standard_normal(out[name].shape)
        drawn = base * np.exp(spread * noise) if base else spread * noise
        out[name] = __import__('jax').numpy.asarray(drawn.astype(out[name].dtype))
    for name, factor in factors.items():
        out[name] = (out[name] * factor).astype(out[name].dtype)
    return out
```

```python
import numpy as np
import concourse.bass as bass
from concourse import mybir

F32 = mybir.dt.float32
F32R = mybir.dt.float32r
I32 = mybir.dt.int32
ALU = mybir.AluOpType
ACT = mybir.ActivationFunctionType
AX_X = mybir.AxisListType.X
ds = bass.ds

P = 128
D_MODEL, SEQ, DEC_SEQ, PAST = 2048, 256, 64, 128
DEPTH = 2
TOK = SEQ + DEC_SEQ
KT = D_MODEL // P
KC = 2
CHUNKS = KT // KC
UNIT = 512
BLKS = UNIT // P
D_FF = 4 * D_MODEL
EPS = 1e-5
HEADS, HD = 4, 128
IDX_HEADS, IDX_DIM = 16, 64
C_WIDTH, C_HEADS, C_HD, C_GROUPS, C_STATE, CONV_W = 1024, 16, 64, 4, 128, 4
CONV_DIM = C_WIDTH + 2 * C_GROUPS * C_STATE
XB = CONV_DIM // P
HPG = C_HEADS // C_GROUPS
TILES = ((0, 128), (128, 128), (256, 64))
CTX = CONV_W - 1
CONVIN = CTX + SEQ + CTX + DEC_SEQ
CONVOUT = CONVIN - CTX
CONV_AT = (0, 128, CTX + SEQ)
KEYS = (128, 256, PAST + DEC_SEQ)
TOPK_P = min(256, SEQ // 4)
TOPK_S = min(256, (PAST + DEC_SEQ) // 4)
SCALE = float(HD) ** -0.5
IW_SCALE = float(IDX_DIM) ** -0.5 * float(IDX_HEADS) ** -0.5
NEG = -1e30
NOT_SEEN = -1e38
TAKEN = -3e38
EXT = P - 1 + 257

COL_AQ, COL_AK, COL_AV, COL_IQ = 0, 512, 1024, 1536
COL_IK = 2560
COL_BQ, COL_BK, COL_BV, COL_Z, COL_XBC, COL_DT = 2640, 3152, 3664, 4176, 5200, 7248
PROJ = [("iq", COL_IQ, 0), ("iq", COL_IQ + UNIT, 1), ("small", COL_IK, 0), ("ak", COL_AK, 0), ("aq", COL_AQ, 0),
        ("av", COL_AV, 0), ("bq", COL_BQ, 0), ("bk", COL_BK, 0), ("bv", COL_BV, 0),
        ("xbc", COL_XBC, 0), ("xbc", COL_XBC + UNIT, 1), ("xbc", COL_XBC + 2 * UNIT, 2),
        ("xbc", COL_XBC + 3 * UNIT, 3), ("z", COL_Z, 0), ("z", COL_Z + UNIT, 1)]
Q_OUT = len(PROJ)
N_OUT = D_MODEL // UNIT
Q_MLP = Q_OUT + N_OUT
QUARTERS = D_FF // D_MODEL
N_UP = D_MODEL // UNIT
UNITS = Q_MLP + QUARTERS * 2 * N_UP
Q_SMALL = [k for k, _, _ in PROJ].index("small")
R_IW, R_DT = 64, 96


class Count:

    def __init__(self, nc, name, per, first=0, step=1):
        self.sem, self.per, self.first, self.step = nc.alloc_semaphore(name), per, first, step

    def at(self, layer, k):
        return layer * (self.per * self.step) + (k + self.first) * self.step


class Banks:

    def __init__(self, nc, keys, n=4):
        self.where, use = {}, [0] * n
        for i, key in enumerate(keys):
            self.where[key] = (i % n, use[i % n])
            use[i % n] += 1
        self.filled = [Count(nc, f"mix_bank{b}_filled", use[b]) for b in range(n)]
        self.drained = [Count(nc, f"mix_bank{b}_drained", use[b], first=1) for b in range(n)]

    def bank(self, key):
        return self.where[key][0]


def mixer_fills():
    keys = ["prm", "hist", "ssq0", "sm", "kic"]
    for h in range(IDX_HEADS):
        keys.append(("ip", h))
        if h % 4 == 3:
            keys += [("is", h // 2 - 1), ("is", h // 2)]
    for X in "ab":
        keys.append((X, "kct"))
        for t in range(3):
            keys += [(X, "ktok", t), (X, "vtok", t)]
        for t in range(3):
            keys += [(X, "lg", t, i) for i in range(1 if t == 0 else 2)]
            keys += [(X, "pt", t, i) for i in range(2 if t == 1 else 1)]
            keys.append((X, "pv", t))
    keys += ["last", "acs", "acst", "aend"]
    for t in range(3):
        if t == 2:
            keys += [("si", 0), ("si", 1)]
        keys += [("xt", t, 0), ("xt", t, 1), ("bt", t)]
        for g in range(C_GROUPS):
            keys += [("cb", t, g), ("bc", t, g), ("y", t, g), ("st", t, g)]
        if t:
            keys += [("so", t, 0), ("so", t, 1)]
    keys += [("gs", g) for g in range(C_GROUPS)]
    keys.append("ssq1")
    return keys


def trunk(nc, x_prompt, x_sample, cache_a_k, cache_a_v, cache_a_kidx, cache_b_k, cache_b_v, state_ssm,
          state_conv, norms, w_in, w_out, b_rel_rev, conv_w, conv_b, dt_bias, a_log, d_skip, gate_norm,
          w_up, w_down, ident_in, seen_in, tri_in, rope_in,
          y_prompt, y_sample, p_a_k, p_a_v, p_a_kidx, p_b_k, p_b_v, p_ssm, p_conv,
          s_a_k, s_a_v, s_a_kidx, s_b_k, s_b_v, s_ssm, s_conv):
    def sb(name, shape):
        return nc.alloc_sbuf_tensor(name, shape, F32)

    def twice(name, shape):
        v = sb(name, shape)
        size = 4 * int(np.prod(shape[1:]))
        return v, nc.alloc_sbuf_tensor_at(name + "_parts", shape, F32R, offset=nc.sbuf_base - size)

    def sem(name):
        return nc.alloc_semaphore(name)

    xT = sb("xT", [P, KT, TOK])
    X, X_parts = twice("X", [P, 2, KT, TOK])
    U, U_parts = twice("U", [P, 2, KT, TOK])
    raw, wlo = twice("raw", [P, CHUNKS, KC, UNIT])
    whi = nc.alloc_sbuf_tensor("whi", [P, 4, KC, UNIT], F32R)
    rstd = sb("rstd", [P, TOK])
    TB = sb("TB", [P, BLKS * CONVIN])
    SS4 = sb("SS4", [P, BLKS, TOK])
    ident = sb("ident", [P, P])
    ones = sb("ones", [P, P])
    eps = sb("eps", [P, 1])
    seen = sb("seen", [P, SEQ])
    tri = sb("tri", [P, 2, P])
    ropeA = sb("ropeA", [32, 2, TOK])
    ropeI = sb("ropeI", [P, 2, TOK])
    prm = sb("prm", [P, P])
    dskip = sb("dskip", [P, C_WIDTH // P])
    dtb = sb("dtb", [P, C_HEADS])
    alog = sb("alog", [P, C_HEADS])
    MIX = sb("MIX", [P, KT, TOK])
    XC = sb("XC", [P, XB, CONVOUT])
    TOKS = sb("TOKS", [P, 3, P])
    STD = sb("STD", [P, TOK])
    HIST = sb("HIST", [P, CTX, XB])
    LAST = sb("LAST", [P, 2, CTX, XB])
    DT = sb("DT", [P, 3, C_HEADS])
    ACS = sb("ACS", [P, 3, C_HEADS])
    NACS = sb("NACS", [P, 3, C_HEADS])
    DEND = sb("DEND", [P, 3, C_HEADS])
    SDEC = sb("SDEC", [P, 3, C_HEADS])
    small = sb("small_stats", [P, 64])

    PRM = {"mid": (0, 16), "next": (16, 16), "cw": (32, 64), "cb": (96, 16), "gate": (112, 8)}

    def pcol(what, i):
        return prm[:, PRM[what][0] + i:PRM[what][0] + i + 1]

    AQ, BQ, Z = MIX[:, 0:4, :], MIX[:, 4:8, :], MIX[:, 8:16, :]
    Uf = U[:, :, :, :].rearrange("p a k t -> p (a k t)")
    Xf = X[:, :, :, :].rearrange("p a k t -> p (a k t)")

    def carve(flat):
        at = [0]

        def take(shape):
            n = int(np.prod(shape))
            v = flat[:, at[0]:at[0] + n]
            at[0] += n
            if len(shape) == 2:
                v = v.rearrange("p (a b) -> p a b", b=shape[1])
            if len(shape) == 3:
                v = v.rearrange("p (a b c) -> p a b c", b=shape[1], c=shape[2])
            return v
        return take

    take = carve(Uf)
    AK, AV, BK, BV = take([4, TOK]), take([4, TOK]), take([4, TOK]), take([4, TOK])
    IQ = take([8, TOK])
    VTOK = take([3, UNIT])
    KCT = take([UNIT])
    IKD, IKC = take([TOK]), take([PAST])
    STG = TB[:, 0:2 * UNIT].rearrange("p (a b) -> p a b", a=2)
    take = carve(SS4[:, :, :].rearrange("p b t -> p (b t)"))
    SM, ACST = take([TOK]), take([TOK])[0:C_HEADS]
    tiny = take([7, 3, C_HEADS])
    lrow = take([P])[0:2 * CTX * XB]
    take = carve(Xf)
    PB = take([4, SEQ])
    PT = take([2, UNIT])
    VC = take([UNIT])
    KCt = take([UNIT])
    ABIAS = take([SEQ])
    ABIAS0 = take([P])
    ABIASS = take([PAST + DEC_SEQ])
    BBIAS = take([4, SEQ])
    RP = take([2, 384])
    RS = take([2, 384])
    KIC = take([IDX_DIM])
    take = carve(Xf)
    XD, XDD, BT = take([C_WIDTH]), take([C_WIDTH]), take([UNIT])
    EX, MM = take([2, UNIT]), take([2, UNIT])
    EB, CTS = take([2, UNIT]), take([2, UNIT])
    ST, H0, SO = take([C_WIDTH]), take([8, P]), take([C_WIDTH])
    YT = take([2, P])
    take = carve(Xf)
    SQZ, GSTD = take([2, TOK]), take([C_GROUPS, TOK])
    prow = sb("prow", [P, P])
    hrow = sb("hrow", [CTX * XB, P])

    G = nc.alloc_psum_tensor("G", [P, 4, 512], F32)
    M = nc.alloc_psum_tensor("M", [P, 4, 512], F32)
    bext = nc.dram_tensor("bias_ext", (DEPTH, P, HEADS, EXT), F32, kind="Internal").ap()
    toeplitz = nc.dram_tensor("bias_toeplitz", (DEPTH, P, HEADS, SEQ), F32, kind="Internal").ap()

    banks = Banks(nc, mixer_fills())

    def mb(key):
        return M[:, banks.bank(key), :]

    raw_in = [Count(nc, f"raw_in{c}", UNITS + 1, step=16) for c in range(CHUNKS)]
    chunk_used = Count(nc, "chunk_used", UNITS * CHUNKS, first=CHUNKS)
    split_done = Count(nc, "split_done", UNITS * CHUNKS)
    low_pair_done = Count(nc, "low_pair_done", UNITS - 1)
    low_free = Count(nc, "low_free", UNITS, first=1)
    high_free = Count(nc, "high_free", UNITS - 1, first=1)
    x_in = Count(nc, "x_in_ready", 4, first=4)
    x_mix = Count(nc, "x_mix_ready", 4)
    x_mid = Count(nc, "x_mid_ready", 4)
    u_ready = Count(nc, "u_ready", 4 * QUARTERS)
    res_new = Count(nc, "residual_new", 8)
    sq_done = Count(nc, "squares_done", 8, first=4)
    ss_done = Count(nc, "sums_done", 8, first=4)
    std_done = Count(nc, "std_done", 2)
    rstd_new = Count(nc, "rstd_new", 2)
    relu_new = Count(nc, "relu_new", 8 * QUARTERS)
    usq_new = Count(nc, "usq_new", 8 * QUARTERS)
    init_in = sem("init_in")
    consts_in = sem("consts_in")
    ones_set = sem("ones_set")
    init_full = [sem(f"init_full{b}") for b in range(4)]
    init_free = [sem(f"init_free{b}") for b in range(4)]
    xT_filled = sem("xT_filled")

    prm_in = Count(nc, "params_in", 9, step=16)
    prm_ready = Count(nc, "params_ready", 2, first=1)
    conv_in = Count(nc, "conv_in", 4)
    conv_tap = Count(nc, "conv_tap", 4)
    conv_out = Count(nc, "conv_out", 4)
    xc_ready = Count(nc, "xc_ready", 4)
    z_new = Count(nc, "z_new", 2)
    z_ready = Count(nc, "z_ready", 2)
    proj_out = Count(nc, "proj_out", 8)
    toks = Count(nc, "toks_ready", 1)
    ikc = Count(nc, "ikc_ready", 1)
    ikd = Count(nc, "ikd_ready", 1)
    cache_in = Count(nc, "cache_in", 4, step=16)
    kidx_out = Count(nc, "indexer_keys_stored", 2, step=16)
    cache_b_in = Count(nc, "cache_b_in", 2, step=16)
    x_free = Count(nc, "x_region_free", 1)
    relu_idx = Count(nc, "relu_idx", 24)
    idx_sum = Count(nc, "idx_sum", 24)
    tok_out = Count(nc, "token_rows_ready", 12)
    rows_out = [Count(nc, "key_rows0_stored", 4, step=16), Count(nc, "key_rows1_stored", 2, step=16)]
    v_out = Count(nc, "value_rows_stored", 6, step=16)
    vt_ready = Count(nc, "v_tokens_ready", 2)
    kct_ready = Count(nc, "kct_ready", 2)
    att_max = Count(nc, "att_max", 6)
    att_exp = Count(nc, "att_exp", 6)
    att_p = Count(nc, "att_p", 6)
    att_pt = Count(nc, "att_pt", 6)
    att_out = Count(nc, "att_out", 6)
    att_done = Count(nc, "att_done", 1)
    last_in = Count(nc, "last_rows", 4)
    lrow_ready = Count(nc, "lrow_ready", 1)
    lrow_out = Count(nc, "lrow_stored", 2, step=16)
    ad_ready = Count(nc, "ad_ready", 1)
    dt_exp = Count(nc, "dt_exp", 1)
    dt_u = Count(nc, "dt_u", 1)
    dt_ln = Count(nc, "dt_ln", 1)
    dt_done = Count(nc, "dt_log_ready", 1)
    acs_ready = Count(nc, "acs_ready", 1)
    acst_ready = Count(nc, "acst_ready", 1)
    dend_in = Count(nc, "dend_in", 1)
    dend_ready = Count(nc, "dend_ready", 1)
    xd_ready = Count(nc, "xd_ready", 3)
    bt_ready = Count(nc, "bt_ready", 3)
    diff = Count(nc, "decay_logs", 12)
    ex_ready = Count(nc, "decays", 12)
    mm_ready = Count(nc, "mm_ready", 12)
    cts_ready = Count(nc, "cts_ready", 12)
    st_ready = Count(nc, "state_ready", 12)
    st_in = Count(nc, "state_loaded", 1, step=16)
    st_first = Count(nc, "state_first", 1)
    so_ready = Count(nc, "state_rows_ready", 2)
    so_out = Count(nc, "state_rows_stored", 2, step=16)
    gz = Count(nc, "gated", 1)
    gsq = Count(nc, "gate_squares", 4)
    gstd = Count(nc, "gate_std", 4)
    bb_ready = Count(nc, "band_bias_ready", 1)
    passed = sem("waits_passed")
    bext_in = sem("bias_rows_in")
    ext_ready = sem("bias_ext_ready")
    bext_out = sem("bias_ext_written")
    toeplitz_in = sem("bias_toeplitz_written")
    fin_ss = sem("final_sums")
    fin_std = sem("final_std")
    fin_new = sem("final_new")
    fin_full = [sem(f"fin_full{b}") for b in range(4)]
    fin_row = sem("final_row")
    fin_out = sem("final_stored")
    layer_a = Count(nc, "act_layer_done", 1, first=1)
    layer_v = Count(nc, "dve_layer_done", 1, first=1)

    def filled(eng, l, key):
        b, n = banks.where[key]
        eng.wait_ge(banks.filled[b].sem, banks.filled[b].at(l, n + 1))

    def apart(eng):
        eng.sem_inc(passed, 1)

    def done_filling(mm, key):
        mm.then_inc(banks.filled[banks.bank(key)].sem, 1)

    def free_bank(pe, l, key):
        b, n = banks.where[key]
        pe.wait_ge(banks.drained[b].sem, banks.drained[b].at(l, n))

    def drained(ins, key):
        ins.then_inc(banks.drained[banks.bank(key)].sem, 1)

    block = nc.Block()
    block.__enter__()

    @block.sync
    def _(sp):
        def load(l, q, c, src):
            sp.wait_ge(chunk_used.sem, chunk_used.at(l, CHUNKS * q + c + 1 - CHUNKS))
            if c == 0:
                apart(sp)
            sp.dma_start(raw[:, c, :, :], src).then_inc(raw_in[c].sem, 16)

        def rows(w, l, row, col):
            return w[ds(l, 1), ds(row, KC * P), ds(col, UNIT)].rearrange("a (k p) n -> p (a k) n", p=P)

        with sp.Fori(0, DEPTH) as l:
            for q, (kind, col, _) in enumerate(PROJ):
                for c in range(CHUNKS):
                    r = slice(c * KC * P, (c + 1) * KC * P)
                    if kind != "small":
                        load(l, q, c, w_in[ds(l, 1), r, col:col + UNIT].rearrange("a (k p) n -> p (a k) n", p=P))
                        continue
                    sp.wait_ge(chunk_used.sem, chunk_used.at(l, CHUNKS * q + c + 1 - CHUNKS))
                    sp.dma_start(raw[:, c, :, 0:R_IW + IDX_HEADS],
                                 w_in[ds(l, 1), r, col:col + R_IW + IDX_HEADS].rearrange("a (k p) n -> p (a k) n", p=P))\
                        .then_inc(raw_in[c].sem, 16)
                    sp.dma_start(raw[:, c, :, R_DT:R_DT + C_HEADS],
                                 w_in[ds(l, 1), r, COL_DT:COL_DT + C_HEADS].rearrange("a (k p) n -> p (a k) n", p=P))\
                        .then_inc(raw_in[c].sem, 16)
            with sp.Fori(0, N_OUT) as j:
                for c in range(CHUNKS):
                    load(l, Q_OUT + j, c, rows(w_out, l, c * KC * P, j * UNIT))
            with sp.Fori(0, QUARTERS) as f:
                with sp.Fori(0, N_UP) as j:
                    for c in range(CHUNKS):
                        load(l, Q_MLP + 2 * N_UP * f + j, c, rows(w_up, l, c * KC * P, f * D_MODEL + j * UNIT))
                with sp.Fori(0, N_UP) as j:
                    for c in range(CHUNKS):
                        load(l, Q_MLP + 2 * N_UP * f + N_UP + j, c, rows(w_down, l, f * D_MODEL + c * KC * P, j * UNIT))

    @block.gpsimd
    def _(pool):
        pool.dma_start(ident[:], ident_in).then_inc(consts_in, 16)
        xin = U[:, :, :, :].rearrange("p a k t -> p (a k t)")
        for t, (o, n) in enumerate(TILES):
            src = x_prompt[0, o:o + n, :] if t < 2 else x_sample[0]
            pool.dma_start(xin[0:n, t * D_MODEL:(t + 1) * D_MODEL], src).then_inc(init_in, 16)
        lead = P - 1
        ext = Uf[:, 3 * D_MODEL:3 * D_MODEL + DEPTH * HEADS * EXT].rearrange("p (i h e) -> p i h e", i=DEPTH, h=HEADS)
        for i in range(DEPTH):
            pool.dma_start(ext[:, i, :, lead:EXT], b_rel_rev[i:i + 1].broadcast_to([P, HEADS, EXT - lead])).then_inc(bext_in, 16)
        pool.wait_ge(bext_in, DEPTH * 16)
        for i in range(DEPTH):
            pool.tensor_copy(ext[:, i, :, 0:lead], ext[:, i, :, lead:lead + 1].broadcast_to([P, HEADS, lead]))
        pool.drain().then_inc(ext_ready, 1)
        pool.wait_ge(ext_ready, 1)
        for i in range(DEPTH):
            pool.dma_start(bext[i], ext[:, i]).then_inc(bext_out, 16)
        pool.wait_ge(bext_out, DEPTH * 16)
        row = HEADS * EXT
        for i in range(DEPTH):
            src = bass.AP(tensor=bext.tensor, offset=bext.offset + i * P * row + lead,
                          ap=[[row - 1, P], [EXT, HEADS], [1, SEQ]])
            pool.dma_start(toeplitz[i], src).then_inc(toeplitz_in, 16)
        pool.dma_start(prow[0:16, :], norms[0, 0:D_MODEL].rearrange("(k p) -> k p", p=P)).then_inc(consts_in, 16)
        pool.dma_start(seen[:], seen_in).then_inc(consts_in, 16)
        pool.dma_start(tri[:], tri_in).then_inc(consts_in, 16)
        pool.dma_start(ropeA[:], rope_in[0, 0:32]).then_inc(consts_in, 16)
        pool.dma_start(ropeI[:], rope_in[1]).then_inc(consts_in, 16)
        pool.memset(ones[:], 1.0).then_inc(ones_set, 1)
        pool.memset(eps[:], EPS).then_inc(ones_set, 1)
        pool.memset(TOKS[:], 0.0).then_inc(ones_set, 1)
        pool.memset(ACS[:], 0.0).then_inc(ones_set, 1)
        pool.memset(SS4[:], 0.0)
        pool.drain()

        sq = TB[:, 0:BLKS * TOK].rearrange("p (b t) -> p b t", b=BLKS)

        def add_squares(l, k):
            pool.wait_ge(sq_done.sem, sq_done.at(l, k + 1))
            pool.tensor_tensor(SS4[:], SS4[:], sq, ALU.add).then_inc(ss_done.sem, 1)
            pool.drain()

        def clear_sums(l, k):
            pool.wait_ge(std_done.sem, std_done.at(l, k + 1))
            apart(pool)
            pool.memset(SS4[:], 0.0)
            pool.drain()

        for j in range(4):
            pool.wait_ge(sq_done.sem, j + 1)
            pool.tensor_tensor(SS4[:], SS4[:], sq, ALU.add).then_inc(ss_done.sem, 1)
            pool.drain()

        outs = {"ak": (p_a_k, s_a_k), "av": (p_a_v, s_a_v), "bk": (p_b_k, s_b_k), "bv": (p_b_v, s_b_v)}
        pool.wait_ge(toeplitz_in, DEPTH * 16)
        with pool.Fori(0, DEPTH) as l:
            pool.wait_ge(prm_ready.sem, prm_ready.at(l, 0))
            pool.wait_ge(layer_a.sem, layer_a.at(l, 0))
            pool.wait_ge(layer_v.sem, layer_v.at(l, 0))
            apart(pool)

            pool.dma_start(prow[0:16, :], norms[ds(2 * l + 1, 1), :].rearrange("a (k p) -> (a k) p", p=P)).then_inc(prm_in.sem, 16)
            pool.dma_start(prow[16:32, :], norms[ds(2 * l + 2, 1), :].rearrange("a (k p) -> (a k) p", p=P)).then_inc(prm_in.sem, 16)
            pool.dma_start(prow[32:96, :], conv_w[ds(l, 1)].rearrange("a j (k p) -> (a j k) p", p=P)).then_inc(prm_in.sem, 16)
            pool.dma_start(prow[96:112, :], conv_b[ds(l, 1), :].rearrange("a (k p) -> (a k) p", p=P)).then_inc(prm_in.sem, 16)
            pool.dma_start(prow[112:120, :], gate_norm[ds(l, 1), :].rearrange("a (k p) -> (a k) p", p=P)).then_inc(prm_in.sem, 16)
            pool.dma_start(dtb[:], dt_bias[ds(l, 1), :].broadcast_to([P, C_HEADS])).then_inc(prm_in.sem, 16)
            pool.dma_start(alog[:], a_log[ds(l, 1), :].broadcast_to([P, C_HEADS])).then_inc(prm_in.sem, 16)
            pool.dma_start(dskip[:], d_skip[ds(l, 1), :].rearrange("a p k -> p (a k)")).then_inc(prm_in.sem, 16)
            pool.dma_start(hrow[:], state_conv[ds(l, 1), 0].rearrange("a j (k p) -> (a j k) p", p=P)).then_inc(prm_in.sem, 16)

            pool.wait_ge(x_free.sem, x_free.at(l, 1))
            apart(pool)
            pool.dma_start(KIC, cache_a_kidx[ds(l, 1), 0].rearrange("a s d -> s (a d)")).then_inc(cache_in.sem, 16)
            pool.dma_start(KCt, cache_a_k[ds(l, 1), 0].rearrange("a s h d -> s (a h d)")).then_inc(cache_in.sem, 16)
            pool.dma_start(VC, cache_a_v[ds(l, 1), 0].rearrange("a s h d -> s (a h d)")).then_inc(cache_in.sem, 16)
            pool.dma_start(BBIAS, toeplitz[ds(l, 1)].rearrange("a p h k -> p (a h) k")).then_inc(cache_in.sem, 16)

            pool.wait_ge(toks.sem, toks.at(l, 1))
            apart(pool)
            pool.dma_start(p_a_kidx[ds(l, 1), 0].rearrange("a (t s) d -> s (a t) d", s=P), TOKS[:, 0:2, 0:IDX_DIM])\
                .then_inc(kidx_out.sem, 16)
            pool.dma_start(s_a_kidx[ds(l, 1), 0].rearrange("a s d -> s (a d)"), TOKS[0:DEC_SEQ, 2, 0:IDX_DIM])\
                .then_inc(kidx_out.sem, 16)

            def store_rows(l, k, name, t, src, stored):
                pool.wait_ge(tok_out.sem, tok_out.at(l, k + 1))
                apart(pool)
                o, n = TILES[t]
                to = outs[name][t // 2]
                o = 0 if t == 2 else o
                pool.dma_start(to[ds(l, 1), 0, o:o + n].rearrange("a s h d -> s (a h d)"), src[0:n]).then_inc(stored.sem, 16)

            for i, X_ in enumerate("ab"):
                if i:
                    pool.wait_ge(att_out.sem, att_out.at(l, 3))
                    apart(pool)
                    pool.dma_start(KCt, cache_b_k[ds(l, 1), 0].rearrange("a s h d -> s (a h d)")).then_inc(cache_b_in.sem, 16)
                    pool.dma_start(VC, cache_b_v[ds(l, 1), 0].rearrange("a s h d -> s (a h d)")).then_inc(cache_b_in.sem, 16)
                for t in range(3):
                    store_rows(l, 6 * i + 2 * t, X_ + "k", t, STG[:, t % 2, :], rows_out[t % 2])
                    store_rows(l, 6 * i + 2 * t + 1, X_ + "v", t, VTOK[:, t, :], v_out)
            pool.wait_ge(lrow_ready.sem, lrow_ready.at(l, 1))
            apart(pool)
            half = XB * CTX
            pool.dma_start(p_conv[ds(l, 1), 0].rearrange("a r (k p) -> (a r k) p", p=P), lrow[0:half, :]).then_inc(lrow_out.sem, 16)
            pool.dma_start(s_conv[ds(l, 1), 0].rearrange("a r (k p) -> (a r k) p", p=P), lrow[half:2 * half, :]).then_inc(lrow_out.sem, 16)
            pool.wait_ge(att_done.sem, att_done.at(l, 1))
            apart(pool)
            pool.dma_start(H0, state_ssm[ds(l, 1), 0].rearrange("a (k h) p n -> (h p) (a k) n", h=2)).then_inc(st_in.sem, 16)
            for i, to in enumerate((p_ssm, s_ssm)):
                pool.wait_ge(so_ready.sem, so_ready.at(l, i + 1))
                apart(pool)
                pool.dma_start(to[ds(l, 1), 0].rearrange("a (k h) p n -> (h p) (a k) n", h=2),
                               SO.rearrange("p (k n) -> p k n", n=P)).then_inc(so_out.sem, 16)
            clear_sums(l, 0)
            for j in range(4):
                add_squares(l, j)
            clear_sums(l, 1)
            for j in range(4):
                add_squares(l, 4 + j)
            pool.wait_ge(kidx_out.sem, kidx_out.at(l, 2))
            pool.wait_ge(lrow_out.sem, lrow_out.at(l, 2))
        for t, (o, n) in enumerate(TILES):
            for i in range(4):
                k = 4 * t + i
                pool.wait_ge(fin_row, k + 1)
                to = y_prompt[0, o:o + n, i * UNIT:(i + 1) * UNIT] if t < 2 else y_sample[0, :, i * UNIT:(i + 1) * UNIT]
                pool.dma_start(to, Uf[0:n, k * UNIT:(k + 1) * UNIT]).then_inc(fin_out, 16)
        pool.wait_ge(fin_out, 12 * 16)
        for stored in rows_out + [v_out]:
            pool.wait_ge(stored.sem, stored.at(DEPTH, 0))
        pool.wait_ge(lrow_out.sem, lrow_out.at(DEPTH, 0))
        pool.wait_ge(so_out.sem, so_out.at(DEPTH, 0))
        pool.wait_ge(kidx_out.sem, kidx_out.at(DEPTH, 0))

    @block.tensor
    def _(pe):
        def unit(l, q, opnd, ready, ready_k, hook=None):
            for c in range(CHUNKS):
                if hook and c == 4:
                    hook()
                pe.wait_ge(split_done.sem, split_done.at(l, CHUNKS * q + c + 1))
                if c % 2 == 0:
                    pe.wait_ge(ready.sem, ready.at(l, ready_k + c // 2 + 1 - ready.first) if ready is x_in
                               else ready.at(l, ready_k + c // 2 + 1))
                for b in range(BLKS):
                    if c == 0 and b == 0:
                        pe.wait_ge(low_free.sem, low_free.at(l, q))
                    if c == 0 and b == 2:
                        pe.wait_ge(high_free.sem, high_free.at(l, q - (q > Q_SMALL) if isinstance(q, int) else q - 1))
                    for k in range(KC):
                        kt = KC * c + k
                        cols = slice(b * P, (b + 1) * P)
                        hi, lo = whi[:, c % 4, k, cols], wlo[:, c, k, cols]
                        out = G[:, b, 0:TOK]
                        xh, xl = opnd[:, 0, kt, :], opnd[:, 1, kt, :]
                        pe.matmul(out, hi, xh, start=(kt == 0), stop=False)
                        pe.matmul(out, hi, xl, start=False, stop=False)
                        mm = pe.matmul(out, lo, xh, start=False, stop=(kt == KT - 1))
                    if c == CHUNKS - 1 and b == 1:
                        mm.then_inc(low_pair_done.sem, 1)
                mm.then_inc(chunk_used.sem, 1)

        def small_unit(l, q):
            for c in range(CHUNKS):
                pe.wait_ge(split_done.sem, split_done.at(l, CHUNKS * q + c + 1))
                if c == 0:
                    pe.wait_ge(low_free.sem, low_free.at(l, q))
                for k in range(KC):
                    kt = KC * c + k
                    hi, lo = whi[:, c % 4, k, 0:P], wlo[:, c, k, 0:P]
                    out = G[:, 0, 0:TOK]
                    xh, xl = X_parts[:, 0, kt, :], X_parts[:, 1, kt, :]
                    pe.matmul(out, hi, xh, start=(kt == 0), stop=False)
                    pe.matmul(out, hi, xl, start=False, stop=False)
                    mm = pe.matmul(out, lo, xh, start=False, stop=(kt == KT - 1))
                mm.then_inc(chunk_used.sem, 1)

        def sum_squares(l, k, key):
            pe.wait_ge(ss_done.sem, ss_done.at(l, 4 * k) if k else ss_done.at(l, 0))
            free_bank(pe, l, key)
            for b in range(BLKS):
                mm = pe.matmul(mb(key)[:, 0:TOK], ones[:], SS4[:, b, :], start=(b == 0), stop=(b == BLKS - 1))
            done_filling(mm, key)

        def transposes(l, key, pieces):
            free_bank(pe, l, key)
            if tuple(pieces[0][1].shape) != (P, P):
                apart(pe)
            for out, in_ in pieces:
                mm = pe.transpose(out, in_, ident[0:in_.shape[0], 0:in_.shape[0]])
            done_filling(mm, key)

        pe.sem_inc(chunk_used.sem, CHUNKS)
        pe.wait_ge(consts_in, 16 * 6)
        pe.wait_ge(ones_set, 4)
        pe.wait_ge(init_in, 16 * 3)
        k = 0
        for t, (o, n) in enumerate(TILES):
            for i in range(4):
                if k >= 4:
                    pe.wait_ge(init_free[k % 4], k // 4)
                for b in range(4):
                    f = t * D_MODEL + (4 * i + b) * P
                    mm = pe.transpose(M[:, k % 4, b * P:b * P + n], Uf[0:n, f:f + P], ident[0:n, 0:n])
                mm.then_inc(init_full[k % 4], 1)
                k += 1
        pe.wait_ge(init_free[0], 3)
        pe.transpose(M[:, 0, 0:16], prow[0:16, :], ident[0:16, 0:16]).then_inc(init_full[0], 1)
        for b in range(4):
            pe.wait_ge(init_free[b], 4 if b == 0 else 3)

        with pe.Fori(0, DEPTH) as l:
            def early():
                pe.wait_ge(prm_in.sem, prm_in.at(l, 9))
                free_bank(pe, l, "prm")
                mm = pe.transpose(mb("prm")[:, 0:120], prow[0:120, :], ident[0:120, 0:120])
                done_filling(mm, "prm")
                transposes(l, "hist", [(mb("hist")[:, 0:CTX * XB], hrow[:, :])])
                sum_squares(l, 0, "ssq0")

            unit(l, 0, X_parts, x_in, 0, hook=early)
            unit(l, 1, X_parts, x_in, 0)
            small_unit(l, Q_SMALL)
            with pe.Fori(Q_SMALL + 1, Q_OUT) as q:
                unit(l, q, X_parts, x_in, 0)

            pe.wait_ge(proj_out.sem, proj_out.at(l, 2))
            transposes(l, "sm", [(mb("sm")[0:n, t * P:(t + 1) * P], SM[:, o:o + n]) for t, (o, n) in enumerate(TILES)])
            pe.wait_ge(cache_in.sem, cache_in.at(l, 4))
            transposes(l, "kic", [(mb("kic")[0:IDX_DIM, 0:P], KIC)])
            pe.wait_ge(ikd.sem, ikd.at(l, 1))
            pe.wait_ge(ikc.sem, ikc.at(l, 1))
            for h in range(IDX_HEADS):
                r = slice(64 * (h % 2), 64 * (h % 2) + 64)
                keys = SM if h % 2 == 0 else IKD
                q = IQ[r, h // 2, :]
                free_bank(pe, l, ("ip", h))
                apart(pe)
                out = mb(("ip", h))
                pe.matmul(out[:, 0:SEQ], q[:, P:SEQ], keys[r, 0:SEQ], start=True, stop=True)
                mm = pe.matmul(out[:, SEQ:SEQ + P], q[:, 0:P], keys[r, 0:P], start=True, stop=True)
                done_filling(mm, ("ip", h))
                if h % 4 != 3:
                    continue
                for odd in range(2):
                    key = ("is", h // 2 - 1 + odd)
                    free_bank(pe, l, key)
                    apart(pe)
                    r = slice(64 * odd, 64 * odd + 64)
                    keys = IKD if odd else SM
                    for i in range(2):
                        out = mb(key)[0:DEC_SEQ, 192 * i:192 * i + 192]
                        q = IQ[r, h // 2 - 1 + i, SEQ:TOK]
                        pe.matmul(out[:, 0:PAST], q, IKC[r, :], start=True, stop=True)
                        mm = pe.matmul(out[:, PAST:192], q, keys[r, SEQ:TOK], start=True, stop=True)
                    done_filling(mm, key)

            for i, (X_, Q, K, V) in enumerate((("a", AQ, AK, AV), ("b", BQ, BK, BV))):
                if i == 0:
                    pe.wait_ge(proj_out.sem, proj_out.at(l, 8))
                else:
                    pe.wait_ge(cache_b_in.sem, cache_b_in.at(l, 2))
                transposes(l, (X_, "kct"), [(mb((X_, "kct"))[:, h * P:(h + 1) * P], KCt[:, h * P:(h + 1) * P])
                                            for h in range(HEADS)])
                for t, (o, n) in enumerate(TILES):
                    for what, src in (("ktok", K), ("vtok", V)):
                        key = (X_, what, t)
                        transposes(l, key, [(mb(key)[0:n, h * P:(h + 1) * P], src[:, h, o:o + n]) for h in range(HEADS)])
                pe.wait_ge(kct_ready.sem, kct_ready.at(l, i + 1))
                pe.wait_ge(vt_ready.sem, vt_ready.at(l, i + 1))
                for t, (o, n) in enumerate(TILES):
                    S = KEYS[t]
                    per = HEADS if t == 0 else 2
                    for j in range(HEADS // per):
                        key = (X_, "lg", t, j)
                        free_bank(pe, l, key)
                        for hh in range(per):
                            h = j * per + hh
                            out = mb(key)[0:n, hh * S:(hh + 1) * S]
                            q = Q[:, h, o:o + n]
                            if t < 2:
                                mm = pe.matmul(out, q, K[:, h, 0:S], start=True, stop=True)
                            else:
                                pe.matmul(out[:, 0:PAST], q, KCT[:, h * P:(h + 1) * P], start=True, stop=True)
                                mm = pe.matmul(out[:, PAST:S], q, K[:, h, o:o + n], start=True, stop=True)
                        done_filling(mm, key)
                    pe.wait_ge(att_p.sem, att_p.at(l, 3 * i + t + 1))
                    if t < 2:
                        for kt in range(S // P):
                            key = (X_, "pt", t, kt)
                            transposes(l, key, [(mb(key)[:, h * P:(h + 1) * P], PB[:, h, kt * P:(kt + 1) * P])
                                                for h in range(HEADS)])
                    else:
                        key = (X_, "pt", t, 0)
                        transposes(l, key, [(mb(key)[:, h * n:(h + 1) * n], PB[0:n, h, 0:PAST]) for h in range(HEADS)]
                                   + [(mb(key)[0:n, 256 + h * n:256 + (h + 1) * n], PB[0:n, h, PAST:S]) for h in range(HEADS)])
                    pe.wait_ge(att_pt.sem, att_pt.at(l, 3 * i + t + 1))
                    key = (X_, "pv", t)
                    free_bank(pe, l, key)
                    for h in range(HEADS):
                        out = mb(key)[:, h * n:(h + 1) * n]
                        vcols = slice(h * P, (h + 1) * P)
                        if t < 2:
                            for kt in range(S // P):
                                mm = pe.matmul(out, VTOK[:, kt, vcols], PT[:, kt, h * P:(h + 1) * P],
                                               start=(kt == 0), stop=(kt == S // P - 1))
                        else:
                            pe.matmul(out, VC[:, vcols], PT[:, 0, h * n:(h + 1) * n], start=True, stop=False)
                            mm = pe.matmul(out, VTOK[0:n, 2, vcols], PT[0:n, 0, 256 + h * n:256 + (h + 1) * n],
                                           start=False, stop=True)
                    done_filling(mm, key)

            pe.wait_ge(last_in.sem, last_in.at(l, 4))
            transposes(l, "last", [(mb("last")[0:XB * 2 * CTX, 0:P], LAST[:, :, :, :].rearrange("p g r k -> p (g r k)"))])
            pe.wait_ge(ad_ready.sem, ad_ready.at(l, 1))
            free_bank(pe, l, "acs")
            for t, (o, n) in enumerate(TILES):
                mm = pe.matmul(mb("acs")[0:n, t * C_HEADS:(t + 1) * C_HEADS], tri[0:n, 1, 0:n], tiny[0:n, 0, t, :],
                               start=True, stop=True)
            done_filling(mm, "acs")
            pe.wait_ge(acs_ready.sem, acs_ready.at(l, 1))
            transposes(l, "acst", [(mb("acst")[0:C_HEADS, o:o + n], ACS[0:n, t, :]) for t, (o, n) in enumerate(TILES)])
            free_bank(pe, l, "aend")
            for t, (o, n) in enumerate(TILES):
                mm = pe.matmul(mb("aend")[:, t * C_HEADS:(t + 1) * C_HEADS], ident[0:n, n - 1:n].broadcast_to([n, P]),
                               ACS[0:n, t, :], start=True, stop=True)
            done_filling(mm, "aend")
            pe.wait_ge(xc_ready.sem, xc_ready.at(l, 4))
            pe.wait_ge(acst_ready.sem, acst_ready.at(l, 1))
            for t, (o, n) in enumerate(TILES):
                at = CONV_AT[t]
                if t == 2:
                    pe.wait_ge(st_in.sem, st_in.at(l, 1))
                    for i in range(2):
                        transposes(l, ("si", i), [(mb(("si", i))[:, b * P:(b + 1) * P], H0[:, 4 * i + b, :]) for b in range(4)])
                for i in range(2):
                    key = ("xt", t, i)
                    transposes(l, key, [(mb(key)[0:n, b * P:(b + 1) * P], XC[:, 4 * i + b, at:at + n]) for b in range(4)])
                key = ("bt", t)
                transposes(l, key, [(mb(key)[0:n, b * P:(b + 1) * P], XC[:, 8 + b, at:at + n]) for b in range(4)])
                pe.wait_ge(xd_ready.sem, xd_ready.at(l, t + 1))
                pe.wait_ge(bt_ready.sem, bt_ready.at(l, t + 1))
                if t == 2:
                    pe.wait_ge(st_first.sem, st_first.at(l, 1))
                for g in range(C_GROUPS):
                    k = 4 * t + g
                    key = ("cb", t, g)
                    free_bank(pe, l, key)
                    mm = pe.matmul(mb(key)[0:n, 0:n], XC[:, 8 + g, at:at + n], XC[:, 12 + g, at:at + n], start=True, stop=True)
                    done_filling(mm, key)
                    key = ("bc", t, g)
                    free_bank(pe, l, key)
                    for j in range(HPG):
                        h = HPG * g + j
                        mm = pe.matmul(mb(key)[:, j * n:(j + 1) * n], ident[0:C_HEADS, h:h + 1].broadcast_to([C_HEADS, P]),
                                       ACST[:, o:o + n], start=True, stop=True)
                    done_filling(mm, key)
                    key = ("y", t, g)
                    free_bank(pe, l, key)
                    pe.wait_ge(mm_ready.sem, mm_ready.at(l, k + 1))
                    if t:
                        pe.wait_ge(cts_ready.sem, cts_ready.at(l, k + 1))
                    for p in range(2):
                        f = (2 * g + p) * P
                        out = mb(key)[:, 2 * p * n:2 * (p + 1) * n]
                        mm = pe.matmul(out, XD[0:n, f:f + P], MM[0:n, k % 2, 2 * p * n:2 * (p + 1) * n], start=True, stop=(t == 0))
                        if t:
                            mm = pe.matmul(out, ST[:, f:f + P], CTS[:, k % 2, 2 * p * n:2 * (p + 1) * n], start=False, stop=True)
                    done_filling(mm, key)
                    key = ("st", t, g)
                    free_bank(pe, l, key)
                    mm = pe.matmul(mb(key)[:, 0:256], BT[0:n, g * P:(g + 1) * P], XDD[0:n, g * 256:(g + 1) * 256],
                                   start=True, stop=True)
                    done_filling(mm, key)
                if t:
                    pe.wait_ge(st_ready.sem, st_ready.at(l, 4 * t + 4))
                    for i in range(2):
                        key = ("so", t, i)
                        transposes(l, key, [(mb(key)[:, b * P:(b + 1) * P], ST[:, (4 * i + b) * P:(4 * i + b + 1) * P]) for b in range(4)])
            for g in range(C_GROUPS):
                pe.wait_ge(gsq.sem, gsq.at(l, g + 1))
                key = ("gs", g)
                free_bank(pe, l, key)
                for b in range(2):
                    mm = pe.matmul(mb(key)[:, 0:TOK], ones[:], SQZ[:, b, :], start=(b == 0), stop=(b == 1))
                done_filling(mm, key)

            with pe.Fori(Q_OUT, Q_MLP) as q:
                unit(l, q, U_parts, x_mix, 0)
            unit(l, Q_MLP, X_parts, x_mid, 0, hook=lambda: sum_squares(l, 1, "ssq1"))
            with pe.Fori(Q_MLP + 1, Q_MLP + N_UP) as q:
                unit(l, q, X_parts, x_mid, 0)
            with pe.Fori(0, N_UP) as j:
                unit(l, Q_MLP + N_UP + j, U_parts, u_ready, 0)
            with pe.Fori(1, QUARTERS) as f:
                with pe.Fori(0, N_UP) as j:
                    unit(l, Q_MLP + 2 * N_UP * f + j, X_parts, x_mid, 0)
                with pe.Fori(0, N_UP) as j:
                    unit(l, Q_MLP + 2 * N_UP * f + N_UP + j, U_parts, u_ready, 4 * f)
        pe.wait_ge(ss_done.sem, ss_done.at(DEPTH, 0))
        for b in range(4):
            pe.wait_ge(banks.drained[b].sem, banks.drained[b].at(DEPTH, 0))
        for b in range(BLKS):
            mm = pe.matmul(M[:, 0, 0:TOK], ones[:], SS4[:, b, :], start=(b == 0), stop=(b == BLKS - 1))
        mm.then_inc(fin_ss, 1)
        k = 0
        for t, (o, n) in enumerate(TILES):
            for i in range(4):
                pe.wait_ge(fin_new, 1)
                if k >= 4:
                    pe.wait_ge(fin_row, k - 3)
                for b in range(4):
                    mm = pe.transpose(M[0:n, k % 4, b * P:(b + 1) * P], xT[:, 4 * i + b, o:o + n], ident[:, :])
                mm.then_inc(fin_full[k % 4], 1)
                k += 1

    @block.scalar
    def _(act):
        def blocks(flat, n):
            return flat.rearrange("p (b t) -> p b t", b=4)[:, :, 0:n]

        def square_and_weigh(j, what):
            act.activation(TB[:, 0:BLKS * TOK].rearrange("p (b t) -> p b t", b=BLKS), xT[:, 4 * j:4 * j + 4, :], ACT.Square)
            for b in range(BLKS):
                kt = 4 * j + b
                ins = act.activation(X[:, 1, kt, :], xT[:, kt, :], ACT.Copy, scale=pcol(what, kt))
            ins.then_inc(sq_done.sem, 1)

        def make_std(l, k, key):
            filled(act, l, key)
            drained(act.activation(STD[:], mb(key)[:, 0:TOK], ACT.Sqrt, scale=1.0 / D_MODEL, bias=eps[:, 0:1]), key)
            act.drain().then_inc(std_done.sem, 1)

        k = 0
        for t, (o, n) in enumerate(TILES):
            for i in range(4):
                act.wait_ge(init_full[k % 4], k // 4 + 1)
                act.activation(xT[:, 4 * i:4 * i + 4, o:o + n], blocks(M[:, k % 4, :], n), ACT.Copy)\
                    .then_inc(init_free[k % 4], 1)
                k += 1
        act.wait_ge(init_full[0], 4)
        act.activation(prm[:, 16:32], M[:, 0, 0:16], ACT.Copy).then_inc(init_free[0], 1)
        act.drain().then_inc(prm_ready.sem, 1)
        act.wait_ge(ones_set, 4)
        for j in range(4):
            if j:
                act.wait_ge(ss_done.sem, j)
            square_and_weigh(j, "next")
        act.sem_inc(layer_a.sem, 1)

        with act.Fori(0, DEPTH) as l:
            filled(act, l, "prm")
            drained(act.activation(prm[:, 0:120], mb("prm")[:, 0:120], ACT.Copy), "prm")
            act.drain().then_inc(prm_ready.sem, 1)
            filled(act, l, "hist")
            drained(act.activation(HIST[:, :, :].rearrange("p j k -> p (j k)"), mb("hist")[:, 0:CTX * XB], ACT.Copy), "hist")
            act.drain().then_inc(prm_ready.sem, 1)
            make_std(l, 0, "ssq0")
            for half in range(4):
                act.wait_ge(conv_in.sem, conv_in.at(l, half + 1))
                xr = TB[:, :].rearrange("p (b t) -> p b t", b=BLKS)
                for b in range(BLKS):
                    kb = 4 * half + b
                    ins = act.activation(XC[:, kb, :], xr[:, b, CTX:CONVIN], ACT.Identity,
                                         scale=pcol("cw", CTX * XB + kb), bias=pcol("cb", kb))
                ins.then_inc(conv_tap.sem, 1)
                act.wait_ge(conv_out.sem, conv_out.at(l, half + 1))
                x4 = XC[:, 4 * half:4 * half + 4, :]
                act.activation(x4, x4, ACT.Silu).then_inc(xc_ready.sem, 1)
            for half in range(2):
                act.wait_ge(z_new.sem, z_new.at(l, half + 1))
                z4 = Z[:, 4 * half:4 * half + 4, :]
                act.activation(z4, z4, ACT.Silu).then_inc(z_ready.sem, 1)
            filled(act, l, "sm")
            sm = mb("sm").rearrange("p (t c) -> p t c", t=4)
            act.activation(TOKS[:, 0:2, 0:P], sm[:, 0:2, :], ACT.Copy)
            drained(act.activation(TOKS[0:DEC_SEQ, 2, 0:P], sm[0:DEC_SEQ, 2, :], ACT.Copy), "sm")
            act.drain().then_inc(toks.sem, 1)
            filled(act, l, "kic")
            act.activation(IKC[0:64, :], mb("kic")[0:64, 0:P], ACT.Copy)
            drained(act.activation(IKC[64:128, :], mb("kic")[0:64, 0:P], ACT.Copy), "kic")
            act.drain().then_inc(ikc.sem, 1)
            act.wait_ge(x_free.sem, x_free.at(l, 1))
            for h in range(IDX_HEADS):
                if h >= 2:
                    act.wait_ge(idx_sum.sem, idx_sum.at(l, (h - 2) + 2 * ((h - 2) // 4) + 1))
                filled(act, l, ("ip", h))
                drained(act.activation(RP[:, h % 2, :], mb(("ip", h))[:, 0:384], ACT.Relu), ("ip", h))
                act.drain().then_inc(relu_idx.sem, 1)
                if h % 4 == 3:
                    if h >= 7:
                        act.wait_ge(idx_sum.sem, idx_sum.at(l, 6 * (h // 4)))
                    for odd in range(2):
                        key = ("is", h // 2 - 1 + odd)
                        filled(act, l, key)
                        drained(act.activation(RS[0:DEC_SEQ, odd, :], mb(key)[0:DEC_SEQ, 0:384], ACT.Relu), key)
                        act.drain().then_inc(relu_idx.sem, 1)
            for i, (X_, Q) in enumerate((("a", AQ), ("b", BQ))):
                key = (X_, "kct")
                filled(act, l, key)
                drained(act.activation(KCT, mb(key), ACT.Copy), key)
                act.drain().then_inc(kct_ready.sem, 1)
                for t, (o, n) in enumerate(TILES):
                    for w, (what, to) in enumerate((("ktok", STG[0:n, t % 2, :]), ("vtok", VTOK[0:n, t, :]))):
                        key = (X_, what, t)
                        k = 6 * i + 2 * t + w
                        if w == 0 and (i or t == 2):
                            act.wait_ge(rows_out[t % 2].sem, rows_out[t % 2].at(l, 2 * i + t // 2 if t != 1 else i))
                        if w == 1 and i and t == 0:
                            act.wait_ge(v_out.sem, v_out.at(l, 3))
                        filled(act, l, key)
                        drained(act.activation(to, mb(key)[0:n, :], ACT.Copy), key)
                        act.drain().then_inc(tok_out.sem, 1)
                act.drain().then_inc(vt_ready.sem, 1)
                for t, (o, n) in enumerate(TILES):
                    S = KEYS[t]
                    k = 3 * i + t
                    act.wait_ge(att_max.sem, att_max.at(l, k + 1))
                    for h in range(HEADS):
                        ins = act.activation(PB[0:n, h, 0:S], PB[0:n, h, 0:S], ACT.Exp, bias=small[0:n, 32 + h:33 + h],
                                             scale=1.0, accum_out=small[0:n, 36 + h:37 + h])
                    act.drain().then_inc(att_exp.sem, 1)
                    for kt in range(2 if t == 1 else 1):
                        key = (X_, "pt", t, kt)
                        filled(act, l, key)
                        if t < 2:
                            drained(act.activation(PT[:, kt, :], mb(key), ACT.Copy), key)
                        else:
                            act.activation(PT[:, 0, 0:256], mb(key)[:, 0:256], ACT.Copy)
                            drained(act.activation(PT[0:n, 0, 256:512], mb(key)[0:n, 256:512], ACT.Copy), key)
                    act.drain().then_inc(att_pt.sem, 1)
                    key = (X_, "pv", t)
                    filled(act, l, key)
                    drained(act.activation(Q[:, :, o:o + n], mb(key)[:, 0:4 * n].rearrange("p (h t) -> p h t", h=4),
                                           ACT.Copy), key)
                    act.drain().then_inc(att_out.sem, 1)
            filled(act, l, "last")
            drained(act.activation(lrow, mb("last")[0:2 * CTX * XB, 0:P], ACT.Copy), "last")
            act.drain().then_inc(lrow_ready.sem, 1)
            act.activation(alog[:], alog[:], ACT.Exp)
            act.wait_ge(dt_exp.sem, dt_exp.at(l, 1))
            act.activation(tiny[:, 1, :, :], tiny[:, 1, :, :], ACT.Exp).then_inc(dt_u.sem, 1)
            act.wait_ge(dt_ln.sem, dt_ln.at(l, 1))
            act.activation(tiny[:, 6, :, :], tiny[:, 3, :, :], ACT.Ln).then_inc(dt_done.sem, 1)
            act.wait_ge(dend_in.sem, dend_in.at(l, 1))
            act.activation(SDEC[:], SDEC[:], ACT.Exp)
            act.activation(DEND[:], DEND[:], ACT.Exp).then_inc(dend_ready.sem, 1)
            for t, (o, n) in enumerate(TILES):
                filled(act, l, ("bt", t))
                drained(act.activation(BT[0:n, :], mb(("bt", t))[0:n, :], ACT.Copy), ("bt", t))
                act.drain().then_inc(bt_ready.sem, 1)
                for g in range(C_GROUPS):
                    k = 4 * t + g
                    e_ = EX[0:n, k % 2, 0:HPG * n]
                    act.wait_ge(diff.sem, diff.at(l, k + 1))
                    if t:
                        drained(act.activation(EB[:, k % 2, 0:HPG * n], mb(("bc", t, g))[:, 0:HPG * n], ACT.Exp), ("bc", t, g))
                    act.activation(e_, e_, ACT.Exp).then_inc(ex_ready.sem, 1)
                if t:
                    if t == 2:
                        act.wait_ge(so_out.sem, so_out.at(l, 1))
                    for i in range(2):
                        key = ("so", t, i)
                        filled(act, l, key)
                        drained(act.activation(SO[:, i * UNIT:(i + 1) * UNIT], mb(key), ACT.Copy), key)
                    act.drain().then_inc(so_ready.sem, 1)
            act.wait_ge(gz.sem, gz.at(l, 1))
            for g in range(C_GROUPS):
                act.activation(SQZ, Z[:, 2 * g:2 * g + 2, :], ACT.Square).then_inc(gsq.sem, 1)
                key = ("gs", g)
                filled(act, l, key)
                drained(act.activation(GSTD[:, g, :], mb(key)[:, 0:TOK], ACT.Sqrt, scale=1.0 / (C_WIDTH // C_GROUPS),
                                       bias=eps[:, 0:1]), key)
                act.drain().then_inc(gstd.sem, 1)

            act.wait_ge(so_out.sem, so_out.at(l, 2))
            for stored in rows_out + [v_out]:
                act.wait_ge(stored.sem, stored.at(l, stored.per))
            for j in range(N_OUT):
                act.wait_ge(res_new.sem, res_new.at(l, j + 1))
                act.wait_ge(ss_done.sem, ss_done.at(l, j))
                square_and_weigh(j, "mid")
            make_std(l, 1, "ssq1")

            def square_relu(f, j):
                for p_ in range(2):
                    act.wait_ge(relu_new.sem, relu_new.at(l, 8 * f + 2 * j + p_ + 1))
                    act.activation(U[:, 1, ds(4 * j + 2 * p_, 2), :],
                                   TB[:, 2 * p_ * TOK:(2 * p_ + 2) * TOK].rearrange("p (b t) -> p b t", b=2), ACT.Square)\
                        .then_inc(usq_new.sem, 1)

            with act.Fori(0, QUARTERS) as f:
                with act.Fori(0, N_UP) as j:
                    square_relu(f, j)
            for j in range(N_UP):
                act.wait_ge(res_new.sem, res_new.at(l, 4 + j + 1))
                act.wait_ge(ss_done.sem, ss_done.at(l, 4 + j))
                square_and_weigh(j, "next")
            act.drain().then_inc(layer_a.sem, 1)

        act.wait_ge(fin_ss, 1)
        act.activation(STD[:], M[:, 0, 0:TOK], ACT.Sqrt, scale=1.0 / D_MODEL, bias=eps[:, 0:1]).then_inc(fin_std, 1)
        k = 0
        for t, (o, n) in enumerate(TILES):
            for i in range(4):
                act.wait_ge(fin_full[k % 4], k // 4 + 1)
                act.activation(Uf[0:n, k * UNIT:(k + 1) * UNIT], M[0:n, k % 4, :], ACT.Copy).then_inc(fin_row, 1)
                k += 1

    @block.vector
    def _(dve):
        def split_chunk(l, q, c, cols=UNIT):
            dve.wait_ge(raw_in[c].sem, raw_in[c].at(l, q + 1) if not small_before(q) else raw_in[c].at(l, q + 2))
            dve.wait_ge(chunk_used.sem, chunk_used.at(l, CHUNKS * q + c - 3))
            r, h = raw[:, c, :, 0:cols], whi[:, c % 4, :, 0:cols]
            if cols < UNIT:
                dve.memset(raw[:, c, :, R_IW + IDX_HEADS:R_DT], 0.0)
                dve.memset(raw[:, c, :, R_DT + C_HEADS:P], 0.0)
                dve.drain()
            dve.tensor_copy(h, r)
            dve.drain()
            dve.tensor_tensor(wlo[:, c, :, 0:cols], r, h.bitcast(F32), ALU.subtract).then_inc(split_done.sem, 1)

        def small_before(q):
            return not isinstance(q, int) or q >= Q_SMALL

        def chunks(l, q, first, last, cols=UNIT):
            for c in range(first, last):
                split_chunk(l, q, c, cols)

        def next_unit(l, q, cols=UNIT):
            chunks(l, q + 1, 0, 2, cols)

        def wait_low(l, q):
            dve.wait_ge(low_pair_done.sem, low_pair_done.at(l, q - (q > Q_SMALL) + 1 if isinstance(q, int) else q))

        def wait_high(l, q):
            dve.wait_ge(chunk_used.sem, chunk_used.at(l, CHUNKS * (q + 1)))

        def pair(p):
            return G[:, 2 * p:2 * p + 2, 0:TOK]

        def rb(n=2):
            return rstd[:, :].unsqueeze(1).broadcast_to([P, n, TOK])

        def split_operand(full, parts, tiles):
            dve.tensor_copy(parts[:, 0, tiles, :], full[:, 1, tiles, :])
            dve.drain()
            return dve.tensor_tensor(parts[:, 1, tiles, :], full[:, 1, tiles, :],
                                     parts[:, 0, tiles, :].bitcast(F32), ALU.subtract)

        def make_rstd(l, k):
            dve.wait_ge(std_done.sem, std_done.at(l, k + 1))
            dve.reciprocal(rstd[:], STD[:]).then_inc(rstd_new.sem, 1)
            dve.drain()

        dve.sem_inc(low_free.sem, 1)
        dve.sem_inc(high_free.sem, 1)
        for b in range(4):
            dve.sem_inc(banks.drained[b].sem, 1)
        for j in range(4):
            dve.wait_ge(sq_done.sem, j + 1)
            split_operand(X, X_parts, slice(4 * j, 4 * j + 4)).then_inc(x_in.sem, 1)
        dve.sem_inc(layer_v.sem, 1)
        dve.wait_ge(consts_in, 16 * 6)
        dve.wait_ge(ones_set, 4)

        def rope(l, k, x, tab, rows, n):
            shift = 16 if tab is ropeA else 8
            mask = [(i + shift) % (2 * shift) if i < 2 * shift else i for i in range(32)]
            cos = tab[rows, 0, :].unsqueeze(1).broadcast_to([x.shape[0], n, TOK])
            sin = tab[rows, 1, :].unsqueeze(1).broadcast_to([x.shape[0], n, TOK])
            t = TB[rows, 0:n * TOK].rearrange("p (b t) -> p b t", b=n)
            dve.stream_shuffle(t, x, mask)
            dve.drain()
            dve.tensor_tensor(t, t, sin, ALU.mult)
            dve.tensor_tensor(x, x, cos, ALU.mult)
            dve.drain()
            return dve.tensor_tensor(x, x, t, ALU.add)

        with dve.Fori(0, DEPTH) as l:
            chunks(l, 0, 0, 2)
            for q, (kind, _, half) in enumerate(PROJ):
                last = q == len(PROJ) - 1
                chunks(l, q, 2, CHUNKS, P if kind == "small" else UNIT)
                next_unit(l, q, P if q + 1 == Q_SMALL else UNIT)
                if q == 0:
                    make_rstd(l, 0)
                if kind == "small":
                    wait_high(l, q)
                    dve.tensor_tensor(SM, G[:, 0, 0:TOK], rstd[:], ALU.mult).then_inc(low_free.sem, 1)
                    dve.drain()
                    rope(l, 0, SM[0:32, :].unsqueeze(1), ropeI, slice(0, 32), 1)
                    dve.drain()
                    dve.tensor_copy(IKD[64:128, :], SM[0:64, :]).then_inc(ikd.sem, 1)
                    dve.drain().then_inc(proj_out.sem, 1)
                    continue
                if kind != "xbc":
                    dst = {"iq": IQ[:, 4 * half:4 * half + 4, :], "ak": AK, "aq": AQ, "av": AV, "bq": BQ, "bk": BK,
                           "bv": BV, "z": Z[:, 4 * half:4 * half + 4, :]}[kind]
                    wait_low(l, q)
                    dve.tensor_tensor(dst[:, 0:2, :], pair(0), rb(), ALU.mult).then_inc(low_free.sem, 1)
                    wait_high(l, q)
                    ins = dve.tensor_tensor(dst[:, 2:4, :], pair(1), rb(), ALU.mult)
                    ins.then_inc(high_free.sem, 1)
                    dve.drain()
                    if kind == "iq":
                        ins = rope(l, 0, dst, ropeI, slice(0, P), 4)
                    if kind in ("aq", "ak"):
                        ins = rope(l, 0, dst[0:32], ropeA, slice(0, 32), 4)
                    dve.drain()
                    if kind == "z":
                        dve.drain().then_inc(z_new.sem, 1)
                    elif not (kind == "iq" and half == 0):
                        dve.drain().then_inc(proj_out.sem, 1)
                    continue
                xr = TB[:, :].rearrange("p (b t) -> p b t", b=BLKS)
                dve.memset(xr[:, :, 0:CTX], 0.0)
                if half == 0:
                    dve.wait_ge(prm_ready.sem, prm_ready.at(l, 2))
                f4 = slice(4 * half, 4 * half + 4)
                dve.tensor_copy(xr[:, :, CTX + SEQ:2 * CTX + SEQ], HIST[:, :, f4].rearrange("p j k -> p k j"))
                for p_ in range(2):
                    (wait_low if p_ == 0 else wait_high)(l, q)
                    b2 = slice(2 * p_, 2 * p_ + 2)
                    dve.tensor_tensor(xr[:, b2, CTX:CTX + SEQ], pair(p_)[:, :, 0:SEQ],
                                      rstd[:, 0:SEQ].unsqueeze(1).broadcast_to([P, 2, SEQ]), ALU.mult)
                    dve.tensor_tensor(xr[:, b2, 2 * CTX + SEQ:], pair(p_)[:, :, SEQ:TOK],
                                      rstd[:, SEQ:TOK].unsqueeze(1).broadcast_to([P, 2, DEC_SEQ]), ALU.mult)\
                        .then_inc((low_free if p_ == 0 else high_free).sem, 1)
                dve.drain().then_inc(conv_in.sem, 1)
                dve.tensor_copy(LAST[:, 0, :, f4].rearrange("p r k -> p k r"), xr[:, :, SEQ:SEQ + CTX])
                dve.tensor_copy(LAST[:, 1, :, f4].rearrange("p r k -> p k r"), xr[:, :, CONVIN - CTX:CONVIN])\
                    .then_inc(last_in.sem, 1)
                dve.wait_ge(conv_tap.sem, conv_tap.at(l, half + 1))
                for j in range(CONV_W - 1):
                    for b in range(BLKS):
                        kb = 4 * half + b
                        ins = dve.scalar_tensor_tensor(out=XC[:, kb, :], in0=xr[:, b, j:j + CONVOUT],
                                                       scalar=pcol("cw", j * XB + kb), in1=XC[:, kb, :],
                                                       op0=ALU.mult, op1=ALU.add)
                    if j == CONV_W - 2:
                        ins.then_inc(conv_out.sem, 1)
                    dve.drain()

            dve.wait_ge(chunk_used.sem, chunk_used.at(l, CHUNKS * Q_OUT))
            dve.sem_inc(x_free.sem, 1)

            dve.wait_ge(toks.sem, toks.at(l, 1))
            iw = tiny[:, 5, :, :]
            dve.tensor_scalar(iw, TOKS[:, :, R_IW:R_IW + IDX_HEADS], IW_SCALE, None, ALU.mult)
            dve.drain()
            for h in range(IDX_HEADS):
                k = h + 2 * (h // 4)
                dve.wait_ge(relu_idx.sem, relu_idx.at(l, k + 1))
                r = RP[:, h % 2, :]
                if h == 0:
                    dve.tensor_scalar(ABIAS, r[:, 0:SEQ], iw[:, 1, h:h + 1], None, ALU.mult)
                    dve.tensor_scalar(ABIAS0, r[:, SEQ:384], iw[:, 0, h:h + 1], None, ALU.mult).then_inc(idx_sum.sem, 1)
                else:
                    dve.scalar_tensor_tensor(out=ABIAS, in0=r[:, 0:SEQ], scalar=iw[:, 1, h:h + 1], in1=ABIAS,
                                             op0=ALU.mult, op1=ALU.add)
                    dve.scalar_tensor_tensor(out=ABIAS0, in0=r[:, SEQ:384], scalar=iw[:, 0, h:h + 1], in1=ABIAS0,
                                             op0=ALU.mult, op1=ALU.add).then_inc(idx_sum.sem, 1)
                dve.drain()
                if h % 4 != 3:
                    continue
                acc = ABIASS[0:DEC_SEQ]
                for odd in range(2):
                    dve.wait_ge(relu_idx.sem, relu_idx.at(l, k + 2 + odd))
                    for i in range(2):
                        r = RS[0:DEC_SEQ, odd, 192 * i:192 * i + 192]
                        hh = h - 3 + odd + 2 * i
                        w = iw[0:DEC_SEQ, 2, hh:hh + 1]
                        if hh == 0:
                            ins = dve.tensor_scalar(acc, r, w, None, ALU.mult)
                        else:
                            ins = dve.scalar_tensor_tensor(out=acc, in0=r, scalar=w, in1=acc, op0=ALU.mult, op1=ALU.add)
                        if i == 0:
                            dve.drain()
                    ins.then_inc(idx_sum.sem, 1)
                    dve.drain()

            work = [(ABIAS0, seen[:, P:SEQ], TOPK_P), (ABIAS, seen[:, :], TOPK_P),
                    (ABIASS[0:DEC_SEQ], None, TOPK_S)]
            for w, mask, _ in work[:2]:
                dve.scalar_tensor_tensor(out=w, in0=mask, scalar=NOT_SEEN / NEG, in1=w, op0=ALU.mult, op1=ALU.add)
            dve.drain()
            for r in range(TOPK_P // 8):
                for i, (w, _, topk) in enumerate(work):
                    if 8 * r < topk:
                        dve.max(small[0:w.shape[0], 8 * i:8 * i + 8], w)
                dve.drain()
                for i, (w, _, topk) in enumerate(work):
                    if 8 * r < topk:
                        dve.match_replace(w, small[0:w.shape[0], 8 * i:8 * i + 8], w, TAKEN)
                dve.drain()
            for w, _, _ in work:
                dve.tensor_scalar(w, w, TAKEN, NEG, ALU.not_equal, ALU.mult)
            dve.drain()

            dve.wait_ge(cache_in.sem, cache_in.at(l, 4))
            dve.tensor_tensor(BBIAS, BBIAS, seen[:, :].unsqueeze(1).broadcast_to([P, HEADS, SEQ]), ALU.add)
            dve.drain()
            for i, X_ in enumerate("ab"):
                for t, (o, n) in enumerate(TILES):
                    S = KEYS[t]
                    per = HEADS if t == 0 else 2
                    for j in range(HEADS // per):
                        key = (X_, "lg", t, j)
                        filled(dve, l, key)
                        if X_ == "a":
                            bias = ((ABIAS0, ABIAS, ABIASS)[t][0:n]).unsqueeze(1).broadcast_to([n, per, S])
                        else:
                            at = P if t == 0 else 0
                            bias = BBIAS[0:n, j * per:(j + 1) * per, at:at + S]
                        drained(dve.scalar_tensor_tensor(
                            out=PB[0:n, j * per:(j + 1) * per, 0:S],
                            in0=mb(key)[0:n, 0:per * S].rearrange("p (h s) -> p h s", h=per),
                            scalar=SCALE, in1=bias, op0=ALU.mult, op1=ALU.add), key)
                    dve.drain()
                    dve.tensor_reduce(small[0:n, 32:36], PB[0:n, :, 0:S], AX_X, ALU.max, negate=True)\
                        .then_inc(att_max.sem, 1)
                    dve.wait_ge(att_exp.sem, att_exp.at(l, 3 * i + t + 1))
                    dve.reciprocal(small[0:n, 40:44], small[0:n, 36:40])
                    dve.drain()
                    for h in range(HEADS):
                        ins = dve.tensor_scalar(PB[0:n, h, 0:S], PB[0:n, h, 0:S], small[0:n, 40 + h:41 + h], None, ALU.mult)
                    ins.then_inc(att_p.sem, 1)
                    dve.wait_ge(att_pt.sem, att_pt.at(l, 3 * i + t + 1))
            dve.wait_ge(att_out.sem, att_out.at(l, 6))
            dve.sem_inc(att_done.sem, 1)

            v, e, c, u, lg = DT[:, :, :], tiny[:, 1, :, :], tiny[:, 2, :, :], tiny[:, 3, :, :], tiny[:, 4, :, :]
            dve.tensor_tensor(v, TOKS[:, :, R_DT:R_DT + C_HEADS], dtb[:, :].unsqueeze(1).broadcast_to([P, 3, C_HEADS]), ALU.add)
            dve.drain()
            dve.scalar_tensor_tensor(out=e, in0=v, scalar=-1.0, in1=v, op0=ALU.mult, op1=ALU.min).then_inc(dt_exp.sem, 1)
            dve.wait_ge(dt_u.sem, dt_u.at(l, 1))
            dve.tensor_scalar(u, e, 1.0, None, ALU.add).then_inc(dt_ln.sem, 1)
            dve.drain()
            dve.tensor_scalar(c, u, -1.0, None, ALU.add)
            dve.reciprocal(lg, u)
            dve.drain()
            dve.tensor_tensor(c, e, c, ALU.subtract)
            dve.drain()
            dve.tensor_tensor(c, c, lg, ALU.mult)
            dve.tensor_scalar(v, v, 0.0, None, ALU.max)
            dve.drain()
            dve.tensor_tensor(v, v, c, ALU.add)
            dve.drain()
            dve.wait_ge(dt_done.sem, dt_done.at(l, 1))
            dve.tensor_tensor(v, v, tiny[:, 6, :, :], ALU.add)
            dve.drain()
            dve.scalar_tensor_tensor(out=tiny[:, 0, :, :], in0=v, scalar=-1.0,
                                     in1=alog[:, :].unsqueeze(1).broadcast_to([P, 3, C_HEADS]),
                                     op0=ALU.mult, op1=ALU.mult).then_inc(ad_ready.sem, 1)
            filled(dve, l, "acs")
            for t, (o, n) in enumerate(TILES):
                dve.tensor_copy(ACS[0:n, t, :], mb("acs")[0:n, t * C_HEADS:(t + 1) * C_HEADS])
            dve.drain().then_inc(acs_ready.sem, 1)
            dve.tensor_scalar(NACS[:], ACS[:], -1.0, None, ALU.mult)
            drained(dve.drain(), "acs")
            filled(dve, l, "acst")
            drained(dve.tensor_copy(ACST[:, :], mb("acst")[0:C_HEADS, 0:TOK]), "acst")
            dve.drain().then_inc(acst_ready.sem, 1)
            filled(dve, l, "aend")
            dve.tensor_copy(SDEC[:], mb("aend")[:, 0:3 * C_HEADS].rearrange("p (t h) -> p t h", t=3))
            drained(dve.tensor_tensor(DEND[:], mb("aend")[:, 0:3 * C_HEADS].rearrange("p (t h) -> p t h", t=3), ACS[:],
                                      ALU.subtract), "aend")
            dve.drain().then_inc(dend_in.sem, 1)
            dve.wait_ge(dend_ready.sem, dend_ready.at(l, 1))

            for t, (o, n) in enumerate(TILES):
                at = CONV_AT[t]
                if t == 2:
                    dve.wait_ge(so_ready.sem, so_ready.at(l, 1))
                    for i in range(2):
                        key = ("si", i)
                        filled(dve, l, key)
                        drained(dve.tensor_copy(ST[:, i * UNIT:(i + 1) * UNIT], mb(key)), key)
                    dve.drain().then_inc(st_first.sem, 1)
                hb = [n, 8, C_HD]
                for i in range(2):
                    key = ("xt", t, i)
                    filled(dve, l, key)
                    drained(dve.tensor_tensor(XD[0:n, i * UNIT:(i + 1) * UNIT].rearrange("p (h d) -> p h d", d=C_HD),
                                              mb(key)[0:n, :].rearrange("p (h d) -> p h d", d=C_HD),
                                              DT[0:n, t, 8 * i:8 * i + 8].unsqueeze(2).broadcast_to(hb), ALU.mult), key)
                dve.drain()
                dve.tensor_tensor(XDD[0:n, :].rearrange("p (h d) -> p h d", d=C_HD),
                                  XD[0:n, :].rearrange("p (h d) -> p h d", d=C_HD),
                                  DEND[0:n, t, :].unsqueeze(2).broadcast_to([n, C_HEADS, C_HD]), ALU.mult)\
                    .then_inc(xd_ready.sem, 1)
                for g in range(C_GROUPS):
                    k = 4 * t + g
                    e_, m_ = EX[0:n, k % 2, 0:HPG * n], MM[0:n, k % 2, 0:HPG * n]
                    eb, ct = EB[:, k % 2, 0:HPG * n], CTS[:, k % 2, 0:HPG * n]
                    filled(dve, l, ("bc", t, g))
                    for j in range(HPG):
                        h = HPG * g + j
                        ins = dve.scalar_tensor_tensor(out=e_[:, j * n:(j + 1) * n],
                                                       in0=mb(("bc", t, g))[0:n, j * n:(j + 1) * n],
                                                       scalar=NACS[0:n, t, h:h + 1], in1=tri[0:n, 0, 0:n],
                                                       op0=ALU.add, op1=ALU.min)
                    ins.then_inc(diff.sem, 1)
                    if t == 0:
                        drained(dve.drain(), ("bc", t, g))
                    dve.wait_ge(ex_ready.sem, ex_ready.at(l, k + 1))
                    key = ("cb", t, g)
                    filled(dve, l, key)
                    ins = dve.tensor_tensor(m_.rearrange("p (j s) -> p j s", j=HPG), e_.rearrange("p (j s) -> p j s", j=HPG),
                                            mb(key)[0:n, 0:n].unsqueeze(1).broadcast_to([n, HPG, n]), ALU.mult)
                    drained(ins, key)
                    dve.drain().then_inc(mm_ready.sem, 1)
                    if t:
                        dve.tensor_tensor(ct.rearrange("p (j s) -> p j s", j=HPG), eb.rearrange("p (j s) -> p j s", j=HPG),
                                          XC[:, 12 + g, at:at + n].unsqueeze(1).broadcast_to([P, HPG, n]), ALU.mult)\
                            .then_inc(cts_ready.sem, 1)
                    else:
                        dve.drain().then_inc(cts_ready.sem, 1)
                    key = ("y", t, g)
                    filled(dve, l, key)
                    for p in range(2):
                        kb = 2 * g + p
                        for half in range(2):
                            r = slice(64 * half, 64 * half + 64)
                            ins = dve.scalar_tensor_tensor(
                                out=YT[r, p, 0:n], in0=XC[r, kb, at:at + n], scalar=dskip[r, kb:kb + 1],
                                in1=mb(key)[r, (2 * p + half) * n:(2 * p + half + 1) * n], op0=ALU.mult, op1=ALU.add)
                    drained(ins, key)
                    dve.drain()
                    if k == 0:
                        dve.wait_ge(z_ready.sem, z_ready.at(l, 2))
                    dve.tensor_tensor(Z[:, 2 * g:2 * g + 2, o:o + n], Z[:, 2 * g:2 * g + 2, o:o + n], YT[:, :, 0:n], ALU.mult)
                    key = ("st", t, g)
                    filled(dve, l, key)
                    s_ = ST[:, g * 256:(g + 1) * 256]
                    if t == 0:
                        drained(dve.tensor_copy(s_, mb(key)[:, 0:256]), key)
                    else:
                        dve.tensor_tensor(s_.rearrange("p (h d) -> p h d", d=C_HD), s_.rearrange("p (h d) -> p h d", d=C_HD),
                                          SDEC[:, t, HPG * g:HPG * g + HPG].unsqueeze(2).broadcast_to([P, HPG, C_HD]), ALU.mult)
                        dve.drain()
                        drained(dve.tensor_tensor(s_, s_, mb(key)[:, 0:256], ALU.add), key)
                    dve.drain().then_inc(st_ready.sem, 1)
            dve.drain().then_inc(gz.sem, 1)
            for g in range(C_GROUPS):
                dve.wait_ge(gstd.sem, gstd.at(l, g + 1))
                gr = GSTD[:, g, :]
                dve.reciprocal(gr, gr)
                dve.drain()
                for b in range(2):
                    zb = Z[:, 2 * g + b, :]
                    dve.scalar_tensor_tensor(out=zb, in0=zb, scalar=pcol("gate", 2 * g + b), in1=gr, op0=ALU.mult, op1=ALU.mult)
            dve.drain()
            for stored in rows_out + [v_out]:
                dve.wait_ge(stored.sem, stored.at(l, stored.per))
            for j in range(4):
                m4 = MIX[:, 4 * j:4 * j + 4, :]
                dve.tensor_copy(U_parts[:, 0, 4 * j:4 * j + 4, :], m4)
                dve.drain()
                dve.tensor_tensor(U_parts[:, 1, 4 * j:4 * j + 4, :], m4,
                                  U_parts[:, 0, 4 * j:4 * j + 4, :].bitcast(F32), ALU.subtract).then_inc(x_mix.sem, 1)

            def add_residual(l, q, j):
                for p_ in range(2):
                    (wait_low if p_ == 0 else wait_high)(l, q)
                    x2 = xT[:, ds(4 * j + 2 * p_, 2), :]
                    ins = dve.tensor_tensor(x2, x2, pair(p_), ALU.add)
                    ins.then_inc((low_free if p_ == 0 else high_free).sem, 1)
                dve.drain()

            def new_operand(l, j, k, ready):
                dve.drain().then_inc(res_new.sem, 1)
                dve.wait_ge(sq_done.sem, sq_done.at(l, k + 1))
                split_operand(X, X_parts, ds(4 * j, 4)).then_inc(ready.sem, 1)

            for j in range(N_OUT):
                q = Q_OUT + j
                chunks(l, q, 2, CHUNKS)
                next_unit(l, q)
                add_residual(l, q, j)
                new_operand(l, j, j, x_mid)

            def relu_half(l, q, kk, p_):
                t2 = TB[:, 2 * p_ * TOK:(2 * p_ + 2) * TOK].rearrange("p (b t) -> p b t", b=2)
                (wait_low if p_ == 0 else wait_high)(l, q)
                ins = dve.scalar_tensor_tensor(out=t2, in0=pair(p_), scalar=0.0, in1=rb(), op0=ALU.max, op1=ALU.mult)
                ins.then_inc((low_free if p_ == 0 else high_free).sem, 1)
                dve.drain().then_inc(relu_new.sem, 1)

            def up_unit(l, q, f, j):
                relu_half(l, q, 0, 0)
                relu_half(l, q, 0, 1)
                for p_ in range(2):
                    dve.wait_ge(usq_new.sem, usq_new.at(l, 8 * f + 2 * j + p_ + 1))
                    ins = split_operand(U, U_parts, ds(4 * j + 2 * p_, 2))
                ins.then_inc(u_ready.sem, 1)

            chunks(l, Q_MLP, 2, CHUNKS)
            next_unit(l, Q_MLP)
            make_rstd(l, 1)
            up_unit(l, Q_MLP, 0, 0)
            with dve.Fori(1, N_UP) as j:
                q = Q_MLP + j
                chunks(l, q, 2, CHUNKS)
                next_unit(l, q)
                up_unit(l, q, 0, j)
            with dve.Fori(1, QUARTERS) as f:
                with dve.Fori(0, N_UP) as j:
                    q = Q_MLP + 2 * N_UP * f - N_UP + j
                    chunks(l, q, 2, CHUNKS)
                    next_unit(l, q)
                    add_residual(l, q, j)
                with dve.Fori(0, N_UP) as j:
                    q = Q_MLP + 2 * N_UP * f + j
                    chunks(l, q, 2, CHUNKS)
                    next_unit(l, q)
                    up_unit(l, q, f, j)
            for j in range(N_UP):
                q = UNITS - N_UP + j
                chunks(l, q, 2, CHUNKS)
                if j < N_UP - 1:
                    next_unit(l, q)
                add_residual(l, q, j)
                new_operand(l, j, 4 + j, x_in)
            dve.drain().then_inc(layer_v.sem, 1)

        dve.wait_ge(fin_std, 1)
        dve.reciprocal(rstd[:], STD[:])
        dve.drain()
        for j in range(4):
            x4 = xT[:, 4 * j:4 * j + 4, :]
            dve.tensor_tensor(x4, X_parts[:, 0, 4 * j:4 * j + 4, :].bitcast(F32), X_parts[:, 1, 4 * j:4 * j + 4, :].bitcast(F32), ALU.add)
            dve.drain()
            ins = dve.tensor_tensor(x4, x4, rb(4), ALU.mult)
        ins.then_inc(fin_new, 1)

    block.__exit__(None, None, None)


def constants():
    f = np.float32
    q, k = np.arange(P)[:, None], np.arange(SEQ)[None]
    seen = np.where(k < P + 64 * (q // 64 + 1), 0, NEG).astype(f)
    s, t = np.arange(P)[:, None], np.arange(P)[None]
    tri = np.stack([np.where(s <= t, 0, NEG), (s <= t)], axis=1).astype(f)
    pos = np.concatenate([np.arange(SEQ), PAST + np.arange(DEC_SEQ)]).astype(f)
    rope = np.zeros((2, P, 2, TOK), f)
    rope[:, :, 0] = 1
    for i, (dim, starts) in enumerate(((HD, (0,)), (IDX_DIM, (0, 64)))):
        rot = dim // 4
        half = rot // 2
        inv = f(500000.0) ** (-np.arange(half, dtype=f) * f(2.0) / f(rot))
        ang = (pos[None, :] * inv[:, None]).astype(f)
        for a in starts:
            for j in (0, half):
                rope[i, a + j:a + j + half, 0] = np.cos(ang)
            rope[i, a:a + half, 1] = -np.sin(ang)
            rope[i, a + half:a + rot, 1] = np.sin(ang)
    return {"ident": np.eye(P, dtype=f), "seen": seen, "tri": tri, "rope": rope}


def kernel(x_prompt, x_sample, cache_a_k, cache_a_v, cache_a_kidx, cache_b_k, cache_b_v, state_ssm, state_conv,
           norm1, w_in, w_out, b_rel, conv_w, conv_b, dt_bias, a_log, d_skip, gate_norm, norm2, w_up, w_down,
           final_norm):
    import concourse.bacc as bacc
    from concourse.bass_utils import run_bass_kernel_spmd

    a = np.ascontiguousarray
    n1, n2, nf = (np.asarray(v) for v in (norm1, norm2, final_norm))
    norms = np.concatenate([v for i in range(DEPTH) for v in (n1[i:i + 1], n2[i:i + 1])] + [nf[None]])
    skip = np.repeat(np.asarray(d_skip), C_HD, axis=1).reshape(DEPTH, C_WIDTH // P, P).transpose(0, 2, 1)
    c = constants()
    ins = dict(x_prompt=x_prompt, x_sample=x_sample, cache_a_k=cache_a_k, cache_a_v=cache_a_v,
               cache_a_kidx=cache_a_kidx, cache_b_k=cache_b_k, cache_b_v=cache_b_v, state_ssm=state_ssm,
               state_conv=state_conv, norms=norms, w_in=w_in, w_out=w_out, b_rel_rev=np.asarray(b_rel)[:, :, ::-1],
               conv_w=conv_w, conv_b=conv_b, dt_bias=dt_bias, a_log=a_log, d_skip=skip, gate_norm=gate_norm,
               w_up=w_up, w_down=w_down, ident=c["ident"], seen=c["seen"], tri=c["tri"], rope=c["rope"])
    kv = (HEADS, HD)
    outs = dict(y_prompt=(1, SEQ, D_MODEL), y_sample=(1, DEC_SEQ, D_MODEL),
                p_a_k=(DEPTH, 1, SEQ) + kv, p_a_v=(DEPTH, 1, SEQ) + kv, p_a_kidx=(DEPTH, 1, SEQ, IDX_DIM),
                p_b_k=(DEPTH, 1, SEQ) + kv, p_b_v=(DEPTH, 1, SEQ) + kv,
                p_ssm=(DEPTH, 1, C_HEADS, C_HD, C_STATE), p_conv=(DEPTH, 1, CTX, CONV_DIM),
                s_a_k=(DEPTH, 1, DEC_SEQ) + kv, s_a_v=(DEPTH, 1, DEC_SEQ) + kv, s_a_kidx=(DEPTH, 1, DEC_SEQ, IDX_DIM),
                s_b_k=(DEPTH, 1, DEC_SEQ) + kv, s_b_v=(DEPTH, 1, DEC_SEQ) + kv,
                s_ssm=(DEPTH, 1, C_HEADS, C_HD, C_STATE), s_conv=(DEPTH, 1, CTX, CONV_DIM))
    nc = bacc.Bacc("TRN2", target_bir_lowering=False, num_devices=1, dynamic_dma_scratch_size=8192)
    arrays, args = {}, []
    for name, v in ins.items():
        arrays["in_" + name] = a(v)
        args.append(nc.dram_tensor("in_" + name, arrays["in_" + name].shape, F32, kind="ExternalInput").ap())
    for name, shape in outs.items():
        args.append(nc.dram_tensor("out_" + name, shape, F32, kind="ExternalOutput").ap())
    trunk(nc, *args)
    r = run_bass_kernel_spmd(nc, [arrays], core_ids=[0])
    return tuple(r.results[0]["out_" + name] for name in outs)
```

```python
import numpy as np
import concourse.bass as bass
from concourse import mybir

F32 = mybir.dt.float32
F32R = mybir.dt.float32r
ALU = mybir.AluOpType
ACT = mybir.ActivationFunctionType
AX_X = mybir.AxisListType.X
ds = bass.ds

P = 128
D_MODEL, SEQ, DEC_SEQ, PAST = 2048, 256, 64, 128
DEPTH = 2
TOK = SEQ + DEC_SEQ
KT = D_MODEL // P
KC = 2
CHUNKS = KT // KC
UNIT = 512
BLKS = UNIT // P
D_FF = 4 * D_MODEL
EPS = 1e-5
HEADS, HD = 4, 128
IDX_HEADS, IDX_DIM = 16, 64
C_WIDTH, C_HEADS, C_HD, C_GROUPS, C_STATE, CONV_W = 1024, 16, 64, 4, 128, 4
CONV_DIM = C_WIDTH + 2 * C_GROUPS * C_STATE
XB = CONV_DIM // P
HPG = C_HEADS // C_GROUPS
TILES = ((0, 128), (128, 128), (256, 64))
CTX = CONV_W - 1
CONVIN = CTX + SEQ + CTX + DEC_SEQ
CONVOUT = CONVIN - CTX
CONV_AT = (0, 128, CTX + SEQ)
KEYS = (128, 256, PAST + DEC_SEQ)
TOPK_P = min(256, SEQ // 4)
TOPK_S = min(256, (PAST + DEC_SEQ) // 4)
SCALE = float(HD) ** -0.5
IW_SCALE = float(IDX_DIM) ** -0.5 * float(IDX_HEADS) ** -0.5
NEG = -1e30
NOT_SEEN = -1e38
TAKEN = -3e38
EXT = P - 1 + 257

COL_AQ, COL_AK, COL_AV, COL_IQ = 0, 512, 1024, 1536
COL_IK = 2560
COL_BQ, COL_BK, COL_BV, COL_Z, COL_XBC, COL_DT = 2640, 3152, 3664, 4176, 5200, 7248
PROJ = [("iq", COL_IQ, 0), ("iq", COL_IQ + UNIT, 1), ("small", COL_IK, 0), ("ak", COL_AK, 0), ("aq", COL_AQ, 0),
        ("av", COL_AV, 0), ("bq", COL_BQ, 0), ("bk", COL_BK, 0), ("bv", COL_BV, 0),
        ("z", COL_Z, 0), ("z", COL_Z + UNIT, 1),
        ("xbc", COL_XBC, 0), ("xbc", COL_XBC + UNIT, 1), ("xbc", COL_XBC + 2 * UNIT, 2),
        ("xbc", COL_XBC + 3 * UNIT, 3)]
Q_OUT = len(PROJ)
N_OUT = D_MODEL // UNIT
HALF = CHUNKS // 2
N_HALF = 2 * N_OUT
Q_MLP = Q_OUT + N_OUT
QUARTERS = D_FF // D_MODEL
N_UP = D_MODEL // UNIT
UNITS = Q_MLP + QUARTERS * 2 * N_UP
MORE = N_HALF - N_OUT
READS = UNITS + MORE
SLOTS_PROJ = Q_OUT * CHUNKS
SLOTS_AB = SLOTS_PROJ + N_OUT * HALF
LAG = 2
Q_SMALL = [k for k, _, _ in PROJ].index("small")
R_IW = IDX_DIM
R_DT = R_IW + IDX_HEADS
SMALL = R_DT + C_HEADS


class Count:

    def __init__(self, nc, name, per, first=0, step=1):
        self.sem, self.per, self.first, self.step = nc.alloc_semaphore(name), per, first, step

    def at(self, layer, k):
        return layer * (self.per * self.step) + (k + self.first) * self.step


def schedule():
    after = lambda q: CHUNKS * (q + 1) + 2
    due = {"prm": CHUNKS * (Q_SMALL + 1), "small": after(Q_SMALL)}
    for h in range(IDX_HEADS):
        due["ip", h] = due["small"] + 2 + h
    last = due["ip", IDX_HEADS - 1]
    due["a", "kct"] = last + 1
    for r in range(TOPK_P // 8):
        due["top", r] = last + 1 + r
    due["chosen"] = last + 1 + TOPK_P // 8
    for X, q in (("a", 5), ("b", 8)):
        if X == "b":
            due["b", "kct"] = due["a", "pv", 2]
        for t in range(3):
            due[X, "tok", t] = after(q) + t
            lg = after(q) + 3 + 4 * t
            due[X, "lg", t], due[X, "p", t], due[X, "pt", t], due[X, "pv", t] = lg, lg + 1, lg + 3, lg + 5
    for i, k in enumerate(("ab", "dt1", "dt2", "ad", "acs", "acst", "aend", "dend")):
        due[k] = due["b", "pv", 2] + 1 + i
    at = SLOTS_PROJ + 3
    due["last"] = due["cb"] = at
    for t in range(3):
        due["tile", t] = at + 5 * t
        for g in range(C_GROUPS):
            due["y", t, g] = at + 5 * t + g + (t < 1)
        due["so", t] = at + 5 * t + 5
    due["gate"] = at + 17
    return due


class Steps:

    def __init__(self, part):
        self.part = part
        self.due = next(part)

    def take(self, slot):
        while self.due is not None and self.due <= slot:
            self.due = next(self.part, None)


class Banks:

    def __init__(self, nc, keys, n=4):
        self.where, use = {}, [0] * n
        for i, key in enumerate(keys):
            self.where[key] = (i % n, use[i % n])
            use[i % n] += 1
        self.filled = [Count(nc, f"mix_bank{b}_filled", use[b]) for b in range(n)]
        self.drained = [Count(nc, f"mix_bank{b}_drained", use[b], first=1) for b in range(n)]

    def bank(self, key):
        return self.where[key][0]


def mixer_fills():
    keys = ["ssq0", "prm", "hist", "sm", "kic"]
    for h in range(IDX_HEADS):
        keys.append(("ip", h))
        if h % 4 == 3:
            keys += [("is", h // 2 - 1), ("is", h // 2)]
    keys.append(("a", "kct"))
    for X in "ab":
        if X == "b":
            keys.append((X, "kct"))
        for t in range(3):
            keys += [(X, "ktok", t), (X, "vtok", t)]
        for t in range(4):
            if t < 3:
                keys += [(X, "lg", t, i) for i in range(1 if t == 0 else 2)]
            if t > 0:
                keys.append((X, "pv", t - 1))
            if t < 3:
                keys += [(X, "pt", t, i) for i in range(2 if t == 1 else 1)]
    keys += ["acs", "acst", "aend"]
    keys += ["last", ("cb", 0, 0), ("bc", 0, 0), ("xt", 0, 0), ("xt", 0, 1), ("bt", 0)]
    groups = [(t, g) for t in range(3) for g in range(C_GROUPS)]
    for k, (t, g) in enumerate(groups):
        if k + 1 < len(groups):
            keys += [("cb",) + groups[k + 1], ("bc",) + groups[k + 1]]
        keys += [("y", t, g), ("st", t, g)]
        if g < C_GROUPS - 1:
            continue
        if t:
            keys += [("so", t, 0), ("so", t, 1)]
        if t == 1:
            keys += [("si", 0), ("si", 1)]
        if t < 2:
            keys += [("xt", t + 1, 0), ("xt", t + 1, 1), ("bt", t + 1)]
    keys += [("gs", g) for g in range(C_GROUPS)]
    keys.append("ssq1")
    return keys


def trunk(nc, x_prompt, x_sample, cache_a_k, cache_a_v, cache_a_kidx, cache_b_k, cache_b_v, state_ssm,
          state_conv, norms, w_in, w_out, b_rel_rev, conv_w, conv_b, dt_bias, a_log, d_skip, gate_norm,
          w_up, w_down, ident_arr, seen_in, tri_in, rope_in,
          y_prompt, y_sample, p_a_k, p_a_v, p_a_kidx, p_b_k, p_b_v, p_ssm, p_conv,
          s_a_k, s_a_v, s_a_kidx, s_b_k, s_b_v, s_ssm, s_conv):
    def sb(name, shape):
        return nc.alloc_sbuf_tensor(name, shape, F32)

    def twice(name, shape):
        v = sb(name, shape)
        size = 4 * int(np.prod(shape[1:]))
        return v, nc.alloc_sbuf_tensor_at(name + "_parts", shape, F32R, offset=nc.sbuf_base - size)

    def sem(name):
        return nc.alloc_semaphore(name)

    xT = sb("xT", [P, KT, TOK])
    X, X_parts = twice("X", [P, 2, KT, TOK])
    U, U_parts = twice("U", [P, 2, KT, TOK])
    raw, wlo = twice("raw", [P, CHUNKS, KC, UNIT])
    whi = nc.alloc_sbuf_tensor("whi", [P, 4, KC, UNIT], F32R)
    rstd = sb("rstd", [P, TOK])
    TB = sb("TB", [P, BLKS * CONVIN])
    SS4 = sb("SS4", [P, BLKS, TOK])
    ident = sb("ident", [P, P])
    ones = sb("ones", [P, P])
    eps = sb("eps", [P, 1])
    seen = sb("seen", [P, SEQ])
    tri = sb("tri", [P, 2, P])
    ropeA = sb("ropeA", [32, 2, TOK])
    ropeI = sb("ropeI", [P, 2, TOK])
    prm = sb("prm", [P, P])
    dskip = sb("dskip", [P, C_WIDTH // P])
    dtb = sb("dtb", [P, C_HEADS])
    alog = sb("alog", [P, C_HEADS])
    MIX = sb("MIX", [P, KT, TOK])
    XC = sb("XC", [P, XB, CONVOUT])
    TOKS = sb("TOKS", [P, 3, P])
    STD = sb("STD", [P, TOK])
    HIST = sb("HIST", [P, CTX, XB])
    LAST = sb("LAST", [P, 2, CTX, XB])
    DT = sb("DT", [P, 3, C_HEADS])
    ACS = sb("ACS", [P, 3, C_HEADS])
    NACS = sb("NACS", [P, 3, C_HEADS])
    DEND = sb("DEND", [P, 3, C_HEADS])
    SDEC = sb("SDEC", [P, 3, C_HEADS])
    small = sb("small_stats", [P, 64])

    PRM = {"mid": (0, 16), "next": (16, 16), "cw": (32, 64), "cb": (96, 16), "gate": (112, 8)}

    def pcol(what, i):
        return prm[:, PRM[what][0] + i:PRM[what][0] + i + 1]

    AQ, BQ, Z = MIX[:, 0:4, :], MIX[:, 4:8, :], MIX[:, 8:16, :]
    Uf = U[:, :, :, :].rearrange("p a k t -> p (a k t)")
    Xf = X[:, :, :, :].rearrange("p a k t -> p (a k t)")

    def carve(flat):
        at = [0]

        def take(shape):
            n = int(np.prod(shape))
            v = flat[:, at[0]:at[0] + n]
            at[0] += n
            if len(shape) == 2:
                v = v.rearrange("p (a b) -> p a b", b=shape[1])
            if len(shape) == 3:
                v = v.rearrange("p (a b c) -> p a b c", b=shape[1], c=shape[2])
            return v
        return take

    take = carve(Uf)
    AK, AV, BK, BV = take([4, TOK]), take([4, TOK]), take([4, TOK]), take([4, TOK])
    IQ = take([8, TOK])
    VTOK = take([3, UNIT])
    KCT = take([UNIT])
    tail = KT * TOK * 2 - UNIT
    IKD, IKC = take([TOK]), take([PAST])
    take = carve(SS4[:, :, :].rearrange("p b t -> p (b t)"))
    SM, ACST = take([TOK]), take([TOK])[0:C_HEADS]
    tiny = take([7, 3, C_HEADS])
    lrow = take([P])[0:2 * CTX * XB]
    take = carve(XC[:, :, :].rearrange("p k t -> p (k t)"))
    RP = take([2, 384])
    RS = take([2, 384])
    PBa, VCa, KCa, KIC = take([4, SEQ]), take([UNIT]), take([UNIT]), take([IDX_DIM])
    ABIAS, ABIAS0, ABIASS = take([SEQ]), take([P]), take([PAST + DEC_SEQ])
    PTa = carve(XC[:, :, :].rearrange("p k t -> p (k t)"))([2, UNIT])
    STGa = TB[:, 0:2 * UNIT].rearrange("p (a b) -> p a b", a=2)
    take = carve(Uf)
    PBb, PTb, stgb0 = take([4, SEQ]), take([2, UNIT]), take([UNIT])
    take = carve(Uf[:, 16 * TOK:24 * TOK])
    VCb, KCb, BBIAS = take([UNIT]), take([UNIT]), take([4, SEQ])
    mixer = {"a": (AQ, AK, AV, KCa, VCa, PBa, PTa, [STGa[:, 0, :], STGa[:, 1, :]]),
             "b": (BQ, BK, BV, KCb, VCb, PBb, PTb, [stgb0, Uf[:, tail:tail + UNIT]])}
    take = carve(Xf)
    XD, XDD, BT = take([C_WIDTH]), take([C_WIDTH]), take([UNIT])
    EX, MM = take([2, UNIT]), take([2, UNIT])
    EB, CTS = take([2, UNIT]), take([2, UNIT])
    ST, H0, SO = take([C_WIDTH]), take([8, P]), take([C_WIDTH])
    YT = take([2, P])
    SQZ = MIX[:, 0:2 * C_GROUPS, :]
    GRMS = TB[:, 0:C_GROUPS * TOK].rearrange("p (g t) -> p g t", g=C_GROUPS)
    prow = sb("prow", [P, P])
    hrow = sb("hrow", [CTX * XB, P])

    G = nc.alloc_psum_tensor("G", [P, 4, 512], F32)
    M = nc.alloc_psum_tensor("M", [P, 4, 512], F32)
    bext = nc.dram_tensor("bias_ext", (DEPTH, P, HEADS, EXT), F32, kind="Internal").ap()
    toeplitz = nc.dram_tensor("bias_toeplitz", (DEPTH, P, HEADS, SEQ), F32, kind="Internal").ap()

    banks = Banks(nc, mixer_fills())

    def mb(key):
        return M[:, banks.bank(key), :]

    raw_in = [Count(nc, f"raw_in{c}", UNITS + 1, step=16) for c in range(CHUNKS)]
    chunk_used = Count(nc, "chunk_used", UNITS * CHUNKS, first=CHUNKS)
    high_done = Count(nc, "high_parts_done", UNITS * CHUNKS)
    split_done = Count(nc, "split_done", UNITS * CHUNKS)
    low_pair_done = Count(nc, "low_pair_done", READS - 1)
    low_free = Count(nc, "low_free", READS, first=1)
    high_free = Count(nc, "high_free", READS - 1, first=1)
    x_in = Count(nc, "x_in_ready", 4, first=4)
    x_mix = Count(nc, "x_mix_ready", 4)
    x_mid = Count(nc, "x_mid_ready", 4)
    u_ready = Count(nc, "u_ready", 4 * QUARTERS)
    res_new = Count(nc, "residual_new", 8, first=1)
    sq_done = Count(nc, "squares_done", 8, first=4)
    ss_done = Count(nc, "sums_done", 8, first=4)
    std_done = Count(nc, "std_done", 2)
    relu_new = Count(nc, "relu_new", 8 * QUARTERS)
    usq_new = Count(nc, "usq_new", 8 * QUARTERS)
    weighed = Count(nc, "residual_weighed", 8, first=4)
    init_in = [sem(f"init_in{t}") for t in range(3)]
    ident_in = sem("ident_in")
    consts_in = sem("consts_in")
    ones_set = sem("ones_set")
    init_full = [sem(f"init_full{b}") for b in range(4)]
    init_free = [sem(f"init_free{b}") for b in range(4)]

    prm_in = Count(nc, "params_in", 9, step=16)
    prm_ready = Count(nc, "params_ready", 2, first=1)
    conv_in = Count(nc, "conv_in", 4)
    conv_tap = Count(nc, "conv_tap", 4)
    conv_out = Count(nc, "conv_out", 4)
    xc_ready = Count(nc, "xc_ready", 4)
    z_new = Count(nc, "z_new", 2)
    z_ready = Count(nc, "z_ready", 2)
    proj_out = Count(nc, "proj_out", 8)
    toks = Count(nc, "toks_ready", 1)
    ikc = Count(nc, "ikc_ready", 1)
    ikd = Count(nc, "ikd_ready", 1)
    cache_in = Count(nc, "cache_in", 3, step=16)
    kidx_out = Count(nc, "indexer_keys_stored", 2, step=16)
    cache_b_in = Count(nc, "cache_b_in", 3, step=16)
    x_free = Count(nc, "x_region_free", 1)
    relu_idx = Count(nc, "relu_idx", 24)
    idx_sum = Count(nc, "idx_sum", 24)
    tok_out = Count(nc, "token_rows_ready", 12)
    rows_out = [Count(nc, "key_rows0_stored", 4, step=16), Count(nc, "key_rows1_stored", 2, step=16)]
    v_out = Count(nc, "value_rows_stored", 6, step=16)
    kct_ready = Count(nc, "kct_ready", 2)
    att_max = Count(nc, "att_max", 6)
    att_exp = Count(nc, "att_exp", 6)
    att_p = Count(nc, "att_p", 6)
    att_pt = Count(nc, "att_pt", 6)
    att_out = Count(nc, "att_out", 6)
    last_in = Count(nc, "last_rows", 4)
    lrow_ready = Count(nc, "lrow_ready", 1)
    lrow_out = Count(nc, "lrow_stored", 2, step=16)
    ad_ready = Count(nc, "ad_ready", 1)
    dt_exp = Count(nc, "dt_exp", 1)
    dt_u = Count(nc, "dt_u", 1)
    dt_ln = Count(nc, "dt_ln", 1)
    dt_done = Count(nc, "dt_log_ready", 1)
    acs_ready = Count(nc, "acs_ready", 1)
    acst_ready = Count(nc, "acst_ready", 1)
    dend_in = Count(nc, "dend_in", 1)
    dend_ready = Count(nc, "dend_ready", 1)
    xd_ready = Count(nc, "xd_ready", 3)
    bt_ready = Count(nc, "bt_ready", 3)
    diff = Count(nc, "decay_logs", 12)
    ex_ready = Count(nc, "decays", 12)
    mm_ready = Count(nc, "mm_ready", 12)
    cts_ready = Count(nc, "cts_ready", 12)
    st_ready = Count(nc, "state_ready", 12)
    st_in = Count(nc, "state_loaded", 1, step=16)
    st_first = Count(nc, "state_first", 1)
    so_ready = Count(nc, "state_rows_ready", 2)
    so_out = Count(nc, "state_rows_stored", 2, step=16)
    gz = Count(nc, "gated", 1)
    gsq = Count(nc, "gate_squares", 4)
    grms = Count(nc, "gate_rms", 4)
    passed = sem("waits_passed")
    bext_in = sem("bias_rows_in")
    ext_ready = sem("bias_ext_ready")
    bext_out = sem("bias_ext_written")
    toeplitz_in = sem("bias_toeplitz_written")
    fin_ss = sem("final_sums")
    fin_std = sem("final_std")
    fin_rstd = sem("final_rstd")
    fin_new = sem("final_new")
    fin_full = sem("final_full")
    fin_row = sem("final_row")
    fin_out = sem("final_stored")
    layer_a = Count(nc, "act_layer_done", 1, first=1)
    layer_v = Count(nc, "dve_layer_done", 1, first=1)

    def filled(eng, l, key):
        b, n = banks.where[key]
        eng.wait_ge(banks.filled[b].sem, banks.filled[b].at(l, n + 1))

    def apart(eng):
        eng.sem_inc(passed, 1)

    def done_filling(mm, key):
        mm.then_inc(banks.filled[banks.bank(key)].sem, 1)

    def free_bank(pe, l, key):
        b, n = banks.where[key]
        pe.wait_ge(banks.drained[b].sem, banks.drained[b].at(l, n))

    def drained(ins, key):
        ins.then_inc(banks.drained[banks.bank(key)].sem, 1)

    due = schedule()
    groups = [(t, g) for t in range(3) for g in range(C_GROUPS)]

    block = nc.Block()
    block.__enter__()

    @block.sync
    def _(sp):
        def load(l, q, c, src):
            sp.wait_ge(chunk_used.sem, chunk_used.at(l, CHUNKS * q + c + 1 - CHUNKS))
            if c == 0:
                apart(sp)
            sp.dma_start(raw[:, c, :, :], src).then_inc(raw_in[c].sem, 16)

        def rows(w, l, row, col):
            return w[ds(l, 1), ds(row, KC * P), ds(col, UNIT)].rearrange("a (k p) n -> p (a k) n", p=P)

        sp.dma_start(ident[:], ident_arr).then_inc(ident_in, 16)
        sp.dma_start(prow[0:16, :], norms[0, 0:D_MODEL].rearrange("(k p) -> k p", p=P)).then_inc(ident_in, 16)
        for t, (o, n) in enumerate(TILES):
            src = x_prompt[0, o:o + n, :] if t < 2 else x_sample[0]
            sp.dma_start(Uf[0:n, t * D_MODEL:(t + 1) * D_MODEL], src).then_inc(init_in[t], 16)
        with sp.Fori(0, DEPTH) as l:
            for q, (kind, col, _) in enumerate(PROJ):
                for c in range(CHUNKS):
                    r = slice(c * KC * P, (c + 1) * KC * P)
                    if kind != "small":
                        load(l, q, c, w_in[ds(l, 1), r, col:col + UNIT].rearrange("a (k p) n -> p (a k) n", p=P))
                        continue
                    sp.wait_ge(chunk_used.sem, chunk_used.at(l, CHUNKS * q + c + 1 - CHUNKS))
                    sp.dma_start(raw[:, c, :, 0:R_IW + IDX_HEADS],
                                 w_in[ds(l, 1), r, col:col + R_IW + IDX_HEADS].rearrange("a (k p) n -> p (a k) n", p=P))\
                        .then_inc(raw_in[c].sem, 16)
                    sp.dma_start(raw[:, c, :, R_DT:R_DT + C_HEADS],
                                 w_in[ds(l, 1), r, COL_DT:COL_DT + C_HEADS].rearrange("a (k p) n -> p (a k) n", p=P))\
                        .then_inc(raw_in[c].sem, 16)
            for top in range(2):
                with sp.Fori(0, N_OUT // 2) as j2:
                    for c in range(CHUNKS):
                        load(l, Q_OUT + top * (N_OUT // 2) + j2, c,
                             rows(w_out, l, (top * HALF + c % HALF) * KC * P, (2 * j2 + c // HALF) * UNIT))
            with sp.Fori(0, QUARTERS) as f:
                with sp.Fori(0, N_UP) as j:
                    for c in range(CHUNKS):
                        load(l, Q_MLP + 2 * N_UP * f + j, c, rows(w_up, l, c * KC * P, f * D_MODEL + j * UNIT))
                with sp.Fori(0, N_UP) as j:
                    for c in range(CHUNKS):
                        load(l, Q_MLP + 2 * N_UP * f + N_UP + j, c, rows(w_down, l, f * D_MODEL + c * KC * P, j * UNIT))

        for k in range(12):
            i, (o, n) = k // 3, TILES[k % 3]
            sp.wait_ge(fin_row, k + 1)
            to = y_prompt[0, o:o + n, i * UNIT:(i + 1) * UNIT] if k % 3 < 2 else y_sample[0, :, i * UNIT:(i + 1) * UNIT]
            sp.dma_start(to, Uf[0:n, k * UNIT:(k + 1) * UNIT]).then_inc(fin_out, 16)
        sp.wait_ge(fin_out, 12 * 16)

    @block.gpsimd
    def _(pool):
        pool.dma_start(seen[:], seen_in).then_inc(consts_in, 16)
        pool.dma_start(tri[:], tri_in).then_inc(consts_in, 16)
        pool.dma_start(ropeA[:], rope_in[0, 0:32]).then_inc(consts_in, 16)
        pool.dma_start(ropeI[:], rope_in[1]).then_inc(consts_in, 16)
        pool.memset(ones[:], 1.0).then_inc(ones_set, 1)
        pool.memset(eps[:], EPS).then_inc(ones_set, 1)
        pool.memset(TOKS[:], 0.0).then_inc(ones_set, 1)
        pool.memset(ACS[:], 0.0).then_inc(ones_set, 1)
        pool.memset(SS4[:], 0.0)
        pool.drain()
        sq = TB[:, 0:BLKS * TOK].rearrange("p (b t) -> p b t", b=BLKS)

        def add_squares(l, k):
            pool.wait_ge(sq_done.sem, sq_done.at(l, k + 1))
            pool.tensor_tensor(SS4[:], SS4[:], sq, ALU.add).then_inc(ss_done.sem, 1)
            pool.drain()

        def clear_sums(l, k):
            pool.wait_ge(std_done.sem, std_done.at(l, k + 1))
            apart(pool)
            pool.memset(SS4[:], 0.0)
            pool.drain()

        pool.wait_ge(prm_ready.sem, 1)
        for j in range(3):
            x4 = xT[:, 4 * j:4 * j + 4, :]
            if j == 0:
                pool.tensor_tensor(SS4[:], x4, x4, ALU.mult).then_inc(ss_done.sem, 1)
                pool.drain()
                continue
            pool.tensor_tensor(sq, x4, x4, ALU.mult)
            pool.drain()
            pool.tensor_tensor(SS4[:], SS4[:], sq, ALU.add).then_inc(ss_done.sem, 1)
            pool.drain()
        pool.wait_ge(sq_done.sem, 4)
        pool.tensor_tensor(SS4[:], SS4[:], sq, ALU.add).then_inc(ss_done.sem, 1)

        lead = P - 1
        ext = XC[:, :, :].rearrange("p k t -> p (k t)")[:, 0:DEPTH * HEADS * EXT].rearrange("p (i h e) -> p i h e", i=DEPTH, h=HEADS)
        for i in range(DEPTH):
            pool.dma_start(ext[:, i, :, lead:EXT], b_rel_rev[i:i + 1].broadcast_to([P, HEADS, EXT - lead])).then_inc(bext_in, 16)
        pool.wait_ge(bext_in, DEPTH * 16)
        for i in range(DEPTH):
            pool.tensor_copy(ext[:, i, :, 0:lead], ext[:, i, :, lead:lead + 1].broadcast_to([P, HEADS, lead]))
        pool.drain().then_inc(ext_ready, 1)
        pool.wait_ge(ext_ready, 1)
        for i in range(DEPTH):
            pool.dma_start(bext[i], ext[:, i]).then_inc(bext_out, 16)
        pool.wait_ge(bext_out, DEPTH * 16)
        row = HEADS * EXT
        for i in range(DEPTH):
            src = bass.AP(tensor=bext.tensor, offset=bext.offset + i * P * row + lead,
                          ap=[[row - 1, P], [EXT, HEADS], [1, SEQ]])
            pool.dma_start(toeplitz[i], src).then_inc(toeplitz_in, 16)

        outs = {"ak": (p_a_k, s_a_k), "av": (p_a_v, s_a_v), "bk": (p_b_k, s_b_k), "bv": (p_b_v, s_b_v)}
        pool.wait_ge(toeplitz_in, DEPTH * 16)
        with pool.Fori(0, DEPTH) as l:
            pool.wait_ge(prm_ready.sem, prm_ready.at(l, 0))
            pool.wait_ge(layer_a.sem, layer_a.at(l, 0))
            pool.wait_ge(layer_v.sem, layer_v.at(l, 0))
            apart(pool)

            pool.dma_start(prow[0:16, :], norms[ds(2 * l + 1, 1), :].rearrange("a (k p) -> (a k) p", p=P)).then_inc(prm_in.sem, 16)
            pool.dma_start(prow[16:32, :], norms[ds(2 * l + 2, 1), :].rearrange("a (k p) -> (a k) p", p=P)).then_inc(prm_in.sem, 16)
            pool.dma_start(prow[32:96, :], conv_w[ds(l, 1)].rearrange("a j (k p) -> (a j k) p", p=P)).then_inc(prm_in.sem, 16)
            pool.dma_start(prow[96:112, :], conv_b[ds(l, 1), :].rearrange("a (k p) -> (a k) p", p=P)).then_inc(prm_in.sem, 16)
            pool.dma_start(prow[112:120, :], gate_norm[ds(l, 1), :].rearrange("a (k p) -> (a k) p", p=P)).then_inc(prm_in.sem, 16)
            pool.dma_start(dtb[:], dt_bias[ds(l, 1), :].broadcast_to([P, C_HEADS])).then_inc(prm_in.sem, 16)
            pool.dma_start(alog[:], a_log[ds(l, 1), :].broadcast_to([P, C_HEADS])).then_inc(prm_in.sem, 16)
            pool.dma_start(dskip[:], d_skip[ds(l, 1), :].rearrange("a p k -> p (a k)")).then_inc(prm_in.sem, 16)
            pool.dma_start(hrow[:], state_conv[ds(l, 1), 0].rearrange("a j (k p) -> (a j k) p", p=P)).then_inc(prm_in.sem, 16)

            pool.dma_start(KIC, cache_a_kidx[ds(l, 1), 0].rearrange("a s d -> s (a d)")).then_inc(cache_in.sem, 16)
            pool.dma_start(KCa, cache_a_k[ds(l, 1), 0].rearrange("a s h d -> s (a h d)")).then_inc(cache_in.sem, 16)
            pool.dma_start(VCa, cache_a_v[ds(l, 1), 0].rearrange("a s h d -> s (a h d)")).then_inc(cache_in.sem, 16)

            pool.wait_ge(toks.sem, toks.at(l, 1))
            apart(pool)
            pool.dma_start(p_a_kidx[ds(l, 1), 0].rearrange("a (t s) d -> s (a t) d", s=P), TOKS[:, 0:2, 0:IDX_DIM])\
                .then_inc(kidx_out.sem, 16)
            pool.dma_start(s_a_kidx[ds(l, 1), 0].rearrange("a s d -> s (a d)"), TOKS[0:DEC_SEQ, 2, 0:IDX_DIM])\
                .then_inc(kidx_out.sem, 16)

            def store_rows(l, k, name, t, src, stored):
                pool.wait_ge(tok_out.sem, tok_out.at(l, k + 1))
                apart(pool)
                o, n = TILES[t]
                to = outs[name][t // 2]
                o = 0 if t == 2 else o
                pool.dma_start(to[ds(l, 1), 0, o:o + n].rearrange("a s h d -> s (a h d)"), src[0:n]).then_inc(stored.sem, 16)

            pool.wait_ge(idx_sum.sem, idx_sum.at(l, idx_sum.per))
            apart(pool)
            pool.dma_start(KCb, cache_b_k[ds(l, 1), 0].rearrange("a s h d -> s (a h d)")).then_inc(cache_b_in.sem, 16)
            pool.dma_start(VCb, cache_b_v[ds(l, 1), 0].rearrange("a s h d -> s (a h d)")).then_inc(cache_b_in.sem, 16)
            pool.dma_start(BBIAS, toeplitz[ds(l, 1)].rearrange("a p h k -> p (a h) k")).then_inc(cache_b_in.sem, 16)
            for i, X_ in enumerate("ab"):
                for t in range(3):
                    store_rows(l, 6 * i + 2 * t, X_ + "k", t, mixer[X_][7][t % 2], rows_out[t % 2])
                    store_rows(l, 6 * i + 2 * t + 1, X_ + "v", t, VTOK[:, t, :], v_out)
            pool.wait_ge(x_free.sem, x_free.at(l, 1))
            apart(pool)
            pool.dma_start(H0, state_ssm[ds(l, 1), 0].rearrange("a (k h) p n -> (h p) (a k) n", h=2)).then_inc(st_in.sem, 16)
            pool.wait_ge(lrow_ready.sem, lrow_ready.at(l, 1))
            apart(pool)
            rows = XB * CTX
            pool.dma_start(p_conv[ds(l, 1), 0].rearrange("a r (k p) -> (a r k) p", p=P), lrow[0:rows, :]).then_inc(lrow_out.sem, 16)
            pool.dma_start(s_conv[ds(l, 1), 0].rearrange("a r (k p) -> (a r k) p", p=P), lrow[rows:2 * rows, :]).then_inc(lrow_out.sem, 16)
            for i, to in enumerate((p_ssm, s_ssm)):
                pool.wait_ge(so_ready.sem, so_ready.at(l, i + 1))
                apart(pool)
                pool.dma_start(to[ds(l, 1), 0].rearrange("a (k h) p n -> (h p) (a k) n", h=2),
                               SO.rearrange("p (k n) -> p k n", n=P)).then_inc(so_out.sem, 16)
            pool.wait_ge(lrow_out.sem, lrow_out.at(l, 2))
            clear_sums(l, 0)
            for j in range(4):
                add_squares(l, j)
            clear_sums(l, 1)
            for j in range(4):
                add_squares(l, 4 + j)
            pool.wait_ge(kidx_out.sem, kidx_out.at(l, 2))
            pool.wait_ge(lrow_out.sem, lrow_out.at(l, 2))
        for stored in rows_out + [v_out]:
            pool.wait_ge(stored.sem, stored.at(DEPTH, 0))
        pool.wait_ge(lrow_out.sem, lrow_out.at(DEPTH, 0))
        pool.wait_ge(so_out.sem, so_out.at(DEPTH, 0))
        pool.wait_ge(kidx_out.sem, kidx_out.at(DEPTH, 0))

    @block.tensor
    def _(pe):
        def unit(l, q, opnd, ready, ready_k, reads=None, part=(0, CHUNKS), ring=0, between=None):
            reads = q if reads is None else reads
            for i, c in enumerate(range(*part)):
                slot = ring + i
                pe.wait_ge(split_done.sem, split_done.at(l, CHUNKS * q + slot + 1))
                if c % 2 == 0:
                    pe.wait_ge(ready.sem, ready.at(l, ready_k + c // 2 + 1 - ready.first))
                for b in range(BLKS):
                    if i == 0 and b == 0:
                        pe.wait_ge(low_free.sem, low_free.at(l, reads))
                    if i == 0 and b == 2:
                        pe.wait_ge(high_free.sem, high_free.at(l, reads - 1 if not isinstance(reads, int) or reads > Q_SMALL
                                                               else reads))
                    for k in range(KC):
                        kt = KC * c + k
                        cols = slice(b * P, (b + 1) * P)
                        hi, lo = whi[:, slot % 4, k, cols], wlo[:, slot, k, cols]
                        out = G[:, b, 0:TOK]
                        xh, xl = opnd[:, 0, kt, :], opnd[:, 1, kt, :]
                        pe.matmul(out, hi, xh, start=(i == 0 and k == 0), stop=False)
                        pe.matmul(out, hi, xl, start=False, stop=False)
                        mm = pe.matmul(out, lo, xh, start=False, stop=(c == part[1] - 1 and k == KC - 1))
                    if c == part[1] - 1 and b == 1:
                        mm.then_inc(low_pair_done.sem, 1)
                mm.then_inc(chunk_used.sem, 1)
                if between:
                    between(CHUNKS * q + slot)

        def small_unit(l, q):
            for c in range(CHUNKS):
                pe.wait_ge(split_done.sem, split_done.at(l, CHUNKS * q + c + 1))
                if c == 0:
                    pe.wait_ge(low_free.sem, low_free.at(l, q))
                for k in range(KC):
                    kt = KC * c + k
                    hi, lo = whi[:, c % 4, k, 0:P], wlo[:, c, k, 0:P]
                    out = G[:, 0, 0:TOK]
                    xh, xl = X_parts[:, 0, kt, :], X_parts[:, 1, kt, :]
                    pe.matmul(out, hi, xh, start=(kt == 0), stop=False)
                    pe.matmul(out, hi, xl, start=False, stop=False)
                    mm = pe.matmul(out, lo, xh, start=False, stop=(kt == KT - 1))
                mm.then_inc(chunk_used.sem, 1)

        def sum_squares(l, k, key):
            pe.wait_ge(ss_done.sem, ss_done.at(l, 4 * k) if k else ss_done.at(l, 0))
            free_bank(pe, l, key)
            for b in range(BLKS):
                mm = pe.matmul(mb(key)[:, 0:TOK], ones[:], SS4[:, b, :], start=(b == 0), stop=(b == BLKS - 1))
            done_filling(mm, key)

        def transposes(l, key, pieces):
            free_bank(pe, l, key)
            if tuple(pieces[0][1].shape) != (P, P):
                apart(pe)
            for out, in_ in pieces:
                mm = pe.transpose(out, in_, ident[0:in_.shape[0], 0:in_.shape[0]])
            done_filling(mm, key)

        pe.sem_inc(chunk_used.sem, CHUNKS)
        pe.wait_ge(ident_in, 16 * 2)
        k = 0
        for t, (o, n) in enumerate(TILES):
            pe.wait_ge(init_in[t], 16)
            for i in range(4):
                if k >= 4:
                    pe.wait_ge(init_free[k % 4], k // 4)
                for b in range(4):
                    f = t * D_MODEL + (4 * i + b) * P
                    mm = pe.transpose(M[:, k % 4, b * P:b * P + n], Uf[0:n, f:f + P], ident[0:n, 0:n])
                mm.then_inc(init_full[k % 4], 1)
                k += 1
        pe.wait_ge(init_free[0], 3)
        pe.transpose(M[:, 0, 0:16], prow[0:16, :], ident[0:16, 0:16]).then_inc(init_full[0], 1)
        for b in range(4):
            pe.wait_ge(init_free[b], 4 if b == 0 else 3)
        pe.wait_ge(consts_in, 16 * 4)
        pe.wait_ge(ones_set, 4)

        with pe.Fori(0, DEPTH) as l:
            def early(slot):
                if slot == 5:
                    sum_squares(l, 0, "ssq0")

            def attention(i, X_):
                Q, K, V, KC_, VC, PB, PT, _ = mixer[X_]
                if i == 1:
                    yield due[X_, "kct"]
                    pe.wait_ge(cache_b_in.sem, cache_b_in.at(l, 3))
                    transposes(l, (X_, "kct"), [(mb((X_, "kct"))[:, h * P:(h + 1) * P], KC_[:, h * P:(h + 1) * P])
                                                for h in range(HEADS)])
                for t, (o, n) in enumerate(TILES):
                    yield due[X_, "tok", t]
                    pe.wait_ge(proj_out.sem, proj_out.at(l, 5 if i == 0 else 8))
                    for what, src in (("ktok", K), ("vtok", V)):
                        key = (X_, what, t)
                        transposes(l, key, [(mb(key)[0:n, h * P:(h + 1) * P], src[:, h, o:o + n]) for h in range(HEADS)])

                def logits(t):
                    o, n = TILES[t]
                    S = KEYS[t]
                    per = HEADS if t == 0 else 2
                    if t == 2:
                        pe.wait_ge(kct_ready.sem, kct_ready.at(l, i + 1))
                    for j in range(HEADS // per):
                        key = (X_, "lg", t, j)
                        free_bank(pe, l, key)
                        for hh in range(per):
                            h = j * per + hh
                            out = mb(key)[0:n, hh * S:(hh + 1) * S]
                            q = Q[:, h, o:o + n]
                            if t < 2:
                                mm = pe.matmul(out, q, K[:, h, 0:S], start=True, stop=True)
                            else:
                                pe.matmul(out[:, 0:PAST], q, KCT[:, h * P:(h + 1) * P], start=True, stop=True)
                                mm = pe.matmul(out[:, PAST:S], q, K[:, h, o:o + n], start=True, stop=True)
                        done_filling(mm, key)

                def weighted(t):
                    o, n = TILES[t]
                    pe.wait_ge(att_pt.sem, att_pt.at(l, 3 * i + t + 1))
                    pe.wait_ge(tok_out.sem, tok_out.at(l, 6 * i + 6))
                    key = (X_, "pv", t)
                    free_bank(pe, l, key)
                    for h in range(HEADS):
                        out = mb(key)[:, h * n:(h + 1) * n]
                        vcols = slice(h * P, (h + 1) * P)
                        if t < 2:
                            for kt in range(KEYS[t] // P):
                                mm = pe.matmul(out, VTOK[:, kt, vcols], PT[:, kt, h * P:(h + 1) * P],
                                               start=(kt == 0), stop=(kt == KEYS[t] // P - 1))
                        else:
                            pe.matmul(out, VC[:, vcols], PT[:, 0, h * n:(h + 1) * n], start=True, stop=False)
                            mm = pe.matmul(out, VTOK[0:n, 2, vcols], PT[0:n, 0, 256 + h * n:256 + (h + 1) * n],
                                           start=False, stop=True)
                    done_filling(mm, key)

                for t in range(4):
                    if t < 3:
                        yield due[X_, "lg", t]
                        logits(t)
                    if t > 0:
                        yield due[X_, "pv", t - 1]
                        weighted(t - 1)
                    if t == 3:
                        continue
                    yield due[X_, "pt", t]
                    o, n = TILES[t]
                    S = KEYS[t]
                    pe.wait_ge(att_p.sem, att_p.at(l, 3 * i + t + 1))
                    if t < 2:
                        for kt in range(S // P):
                            key = (X_, "pt", t, kt)
                            transposes(l, key, [(mb(key)[:, h * P:(h + 1) * P], PB[:, h, kt * P:(kt + 1) * P])
                                                for h in range(HEADS)])
                    else:
                        key = (X_, "pt", t, 0)
                        transposes(l, key, [(mb(key)[:, h * n:(h + 1) * n], PB[0:n, h, 0:PAST]) for h in range(HEADS)]
                                   + [(mb(key)[0:n, 256 + h * n:256 + (h + 1) * n], PB[0:n, h, PAST:S]) for h in range(HEADS)])

            def mixers():
                yield due["prm"]
                pe.wait_ge(prm_in.sem, prm_in.at(l, 9))
                transposes(l, "prm", [(mb("prm")[:, 0:120], prow[0:120, :])])
                transposes(l, "hist", [(mb("hist")[:, 0:CTX * XB], hrow[:, :])])
                yield due["small"]
                pe.wait_ge(proj_out.sem, proj_out.at(l, 2))
                transposes(l, "sm", [(mb("sm")[0:n, t * P:(t + 1) * P], SM[:, o:o + n]) for t, (o, n) in enumerate(TILES)])
                pe.wait_ge(cache_in.sem, cache_in.at(l, 3))
                transposes(l, "kic", [(mb("kic")[0:IDX_DIM, 0:P], KIC)])
                for h in range(IDX_HEADS):
                    yield due["ip", h]
                    if h == 0:
                        pe.wait_ge(ikd.sem, ikd.at(l, 1))
                        pe.wait_ge(ikc.sem, ikc.at(l, 1))
                    r = slice(64 * (h % 2), 64 * (h % 2) + 64)
                    keys = SM if h % 2 == 0 else IKD
                    q = IQ[r, h // 2, :]
                    free_bank(pe, l, ("ip", h))
                    apart(pe)
                    out = mb(("ip", h))
                    pe.matmul(out[:, 0:SEQ], q[:, P:SEQ], keys[r, 0:SEQ], start=True, stop=True)
                    mm = pe.matmul(out[:, SEQ:SEQ + P], q[:, 0:P], keys[r, 0:P], start=True, stop=True)
                    done_filling(mm, ("ip", h))
                    if h % 4 != 3:
                        continue
                    for odd in range(2):
                        key = ("is", h // 2 - 1 + odd)
                        free_bank(pe, l, key)
                        apart(pe)
                        r = slice(64 * odd, 64 * odd + 64)
                        keys = IKD if odd else SM
                        for i in range(2):
                            out = mb(key)[0:DEC_SEQ, 192 * i:192 * i + 192]
                            q = IQ[r, h // 2 - 1 + i, SEQ:TOK]
                            pe.matmul(out[:, 0:PAST], q, IKC[r, :], start=True, stop=True)
                            mm = pe.matmul(out[:, PAST:192], q, keys[r, SEQ:TOK], start=True, stop=True)
                        done_filling(mm, key)
                yield due["a", "kct"]
                transposes(l, ("a", "kct"), [(mb(("a", "kct"))[:, h * P:(h + 1) * P], KCa[:, h * P:(h + 1) * P])
                                             for h in range(HEADS)])
                for i, X_ in enumerate("ab"):
                    yield from attention(i, X_)

                yield due["acs"]
                pe.wait_ge(ad_ready.sem, ad_ready.at(l, 1))
                free_bank(pe, l, "acs")
                for t, (o, n) in enumerate(TILES):
                    mm = pe.matmul(mb("acs")[0:n, t * C_HEADS:(t + 1) * C_HEADS], tri[0:n, 1, 0:n], tiny[0:n, 0, t, :],
                                   start=True, stop=True)
                done_filling(mm, "acs")
                yield due["acst"]
                pe.wait_ge(acs_ready.sem, acs_ready.at(l, 1))
                transposes(l, "acst", [(mb("acst")[0:C_HEADS, o:o + n], ACS[0:n, t, :]) for t, (o, n) in enumerate(TILES)])
                yield due["aend"]
                free_bank(pe, l, "aend")
                for t, (o, n) in enumerate(TILES):
                    mm = pe.matmul(mb("aend")[:, t * C_HEADS:(t + 1) * C_HEADS], ident[0:n, n - 1:n].broadcast_to([n, P]),
                                   ACS[0:n, t, :], start=True, stop=True)
                done_filling(mm, "aend")

                def products(t, g):
                    (o, n), at = TILES[t], CONV_AT[t]
                    key = ("cb", t, g)
                    free_bank(pe, l, key)
                    mm = pe.matmul(mb(key)[0:n, 0:n], XC[:, 8 + g, at:at + n], XC[:, 12 + g, at:at + n], start=True, stop=True)
                    done_filling(mm, key)
                    key = ("bc", t, g)
                    free_bank(pe, l, key)
                    for j in range(HPG):
                        h = HPG * g + j
                        mm = pe.matmul(mb(key)[:, j * n:(j + 1) * n], ident[0:C_HEADS, h:h + 1].broadcast_to([C_HEADS, P]),
                                       ACST[:, o:o + n], start=True, stop=True)
                    done_filling(mm, key)

                def tile(t):
                    (o, n), at = TILES[t], CONV_AT[t]
                    if t == 2:
                        pe.wait_ge(st_in.sem, st_in.at(l, 1))
                        for i in range(2):
                            transposes(l, ("si", i), [(mb(("si", i))[:, b * P:(b + 1) * P], H0[:, 4 * i + b, :]) for b in range(4)])
                    for i in range(2):
                        key = ("xt", t, i)
                        transposes(l, key, [(mb(key)[0:n, b * P:(b + 1) * P], XC[:, 4 * i + b, at:at + n]) for b in range(4)])
                    key = ("bt", t)
                    transposes(l, key, [(mb(key)[0:n, b * P:(b + 1) * P], XC[:, 8 + b, at:at + n]) for b in range(4)])

                def gate():
                    for g in range(C_GROUPS):
                        pe.wait_ge(gsq.sem, gsq.at(l, g + 1))
                        key = ("gs", g)
                        free_bank(pe, l, key)
                        for b in range(2):
                            mm = pe.matmul(mb(key)[:, 0:TOK], ones[:], SQZ[:, 2 * g + b, :], start=(b == 0), stop=(b == 1))
                        done_filling(mm, key)

                yield due["last"]
                pe.wait_ge(last_in.sem, last_in.at(l, 4))
                transposes(l, "last", [(mb("last")[0:XB * 2 * CTX, 0:P], LAST[:, :, :, :].rearrange("p g r k -> p (g r k)"))])
                pe.wait_ge(xc_ready.sem, xc_ready.at(l, 4))
                pe.wait_ge(acst_ready.sem, acst_ready.at(l, 1))
                products(0, 0)
                tile(0)
                for k, (t, g) in enumerate(groups):
                    (o, n), at = TILES[t], CONV_AT[t]
                    yield due["y", t, g]
                    if k + 1 < len(groups):
                        products(*groups[k + 1])
                    if g == 0:
                        pe.wait_ge(xd_ready.sem, xd_ready.at(l, t + 1))
                        pe.wait_ge(bt_ready.sem, bt_ready.at(l, t + 1))
                        if t == 2:
                            pe.wait_ge(st_first.sem, st_first.at(l, 1))
                    key = ("y", t, g)
                    free_bank(pe, l, key)
                    pe.wait_ge(mm_ready.sem, mm_ready.at(l, k + 1))
                    if t:
                        pe.wait_ge(cts_ready.sem, cts_ready.at(l, k + 1))
                    for p in range(2):
                        f = (2 * g + p) * P
                        out = mb(key)[:, 2 * p * n:2 * (p + 1) * n]
                        mm = pe.matmul(out, XD[0:n, f:f + P], MM[0:n, k % 2, 2 * p * n:2 * (p + 1) * n], start=True, stop=(t == 0))
                        if t:
                            mm = pe.matmul(out, ST[:, f:f + P], CTS[:, k % 2, 2 * p * n:2 * (p + 1) * n], start=False, stop=True)
                    done_filling(mm, key)
                    key = ("st", t, g)
                    free_bank(pe, l, key)
                    mm = pe.matmul(mb(key)[:, 0:256], BT[0:n, g * P:(g + 1) * P], XDD[0:n, g * 256:(g + 1) * 256],
                                   start=True, stop=True)
                    done_filling(mm, key)
                    if g < C_GROUPS - 1:
                        continue
                    if t:
                        yield due["so", t]
                        pe.wait_ge(st_ready.sem, st_ready.at(l, 4 * t + 4))
                        for i in range(2):
                            key = ("so", t, i)
                            transposes(l, key, [(mb(key)[:, b * P:(b + 1) * P], ST[:, (4 * i + b) * P:(4 * i + b + 1) * P]) for b in range(4)])
                    if t < 2:
                        yield due["tile", t + 1]
                        tile(t + 1)
                yield due["gate"]
                gate()

            mix = Steps(mixers())
            unit(l, 0, X_parts, x_in, 0, between=early)
            unit(l, 1, X_parts, x_in, 0)
            small_unit(l, Q_SMALL)
            for q in range(Q_SMALL + 1, Q_OUT):
                unit(l, q, X_parts, x_in, 0, between=mix.take)
            for j in range(N_OUT):
                unit(l, Q_OUT + j // 2, U_parts, x_mix, 0, reads=Q_OUT + j, part=(0, HALF), ring=HALF * (j % 2),
                     between=mix.take)
            mix.take(SLOTS_AB + CHUNKS * N_OUT)
            with pe.Fori(0, N_OUT // 2) as j2:
                for j in range(2):
                    unit(l, Q_OUT + N_OUT // 2 + j2, U_parts, x_mix, 0, reads=Q_OUT + N_OUT + 2 * j2 + j,
                         part=(HALF, CHUNKS), ring=HALF * j)

            def mlp(q, opnd, ready, ready_k, between=None):
                unit(l, q, opnd, ready, ready_k, reads=q + MORE, between=between)

            mlp(Q_MLP, X_parts, x_mid, 0, between=lambda slot: slot == CHUNKS * Q_MLP + 5 and sum_squares(l, 1, "ssq1"))
            with pe.Fori(Q_MLP + 1, Q_MLP + N_UP) as q:
                mlp(q, X_parts, x_mid, 0)
            with pe.Fori(0, N_UP) as j:
                mlp(Q_MLP + N_UP + j, U_parts, u_ready, 0)
            with pe.Fori(1, QUARTERS) as f:
                with pe.Fori(0, N_UP) as j:
                    mlp(Q_MLP + 2 * N_UP * f + j, X_parts, x_mid, 0)
                with pe.Fori(0, N_UP) as j:
                    mlp(Q_MLP + 2 * N_UP * f + N_UP + j, U_parts, u_ready, 4 * f)
        for b in range(4):
            pe.wait_ge(banks.drained[b].sem, banks.drained[b].at(DEPTH, 0))
        k = 0
        for i in range(4):
            pe.wait_ge(fin_new, i + 1)
            for t, (o, n) in enumerate(TILES):
                if k >= 3:
                    pe.wait_ge(fin_row, k - 2)
                for b in range(4):
                    mm = pe.transpose(M[0:n, k % 3, b * P:(b + 1) * P], xT[:, 4 * i + b, o:o + n], ident[:, :])
                mm.then_inc(fin_full, 1)
                k += 1
            if i == 0:
                pe.wait_ge(ss_done.sem, ss_done.at(DEPTH, 0))
                for t, (o, n) in enumerate(TILES):
                    for b in range(BLKS):
                        mm = pe.matmul(M[0:n, 3, t:t + 1], SS4[:, b, o:o + n], ones[:, 0:1], start=(b == 0), stop=(b == BLKS - 1))
                mm.then_inc(fin_ss, 1)

    @block.scalar
    def _(act):
        def blocks(flat, n):
            return flat.rearrange("p (b t) -> p b t", b=4)[:, :, 0:n]

        def weigh(j, what):
            for b in range(BLKS):
                kt = 4 * j + b
                ins = act.activation(X[:, 1, kt, :], xT[:, kt, :], ACT.Copy, scale=pcol(what, kt))
            ins.then_inc(weighed.sem, 1)

        def square(j):
            act.activation(TB[:, 0:BLKS * TOK].rearrange("p (b t) -> p b t", b=BLKS), xT[:, 4 * j:4 * j + 4, :], ACT.Square)\
                .then_inc(sq_done.sem, 1)

        def make_std(l, k, key):
            filled(act, l, key)
            drained(act.activation(STD[:], mb(key)[:, 0:TOK], ACT.Sqrt, scale=1.0 / D_MODEL, bias=eps[:, 0:1]), key)
            act.drain().then_inc(std_done.sem, 1)

        k = 0
        for t, (o, n) in enumerate(TILES):
            for i in range(4):
                act.wait_ge(init_full[k % 4], k // 4 + 1)
                act.activation(xT[:, 4 * i:4 * i + 4, o:o + n], blocks(M[:, k % 4, :], n), ACT.Copy)\
                    .then_inc(init_free[k % 4], 1)
                k += 1
        act.wait_ge(init_full[0], 4)
        act.activation(prm[:, 16:32], M[:, 0, 0:16], ACT.Copy).then_inc(init_free[0], 1)
        act.drain().then_inc(prm_ready.sem, 1)
        for j in range(3):
            weigh(j, "next")
        act.wait_ge(ones_set, 4)
        act.sem_inc(sq_done.sem, 3)
        act.sem_inc(layer_a.sem, 1)

        def high_part(l, q, c):
            act.wait_ge(raw_in[c].sem, raw_in[c].at(l, q + 1 if isinstance(q, int) and q < Q_SMALL else q + 2))
            act.wait_ge(chunk_used.sem, chunk_used.at(l, CHUNKS * q + c - 3))
            cols = slice(0, SMALL if isinstance(q, int) and q == Q_SMALL else UNIT)
            act.activation(whi[:, c % 4, :, cols], raw[:, c, :, cols], ACT.Copy).then_inc(high_done.sem, 1)

        def high_parts(l, q, first, last):
            for c in range(first, last):
                high_part(l, q + c // CHUNKS, c % CHUNKS)

        with act.Fori(0, DEPTH) as l:
            high_parts(l, 0, 0, 3)
            act.wait_ge(res_new.sem, res_new.at(l, 0))
            weigh(3, "next")
            act.wait_ge(ss_done.sem, ss_done.at(l, -1))
            square(3)

            def mixers():
                yield due["prm"]
                filled(act, l, "prm")
                drained(act.activation(prm[:, 0:120], mb("prm")[:, 0:120], ACT.Copy), "prm")
                act.drain().then_inc(prm_ready.sem, 1)
                filled(act, l, "hist")
                drained(act.activation(HIST[:, :, :].rearrange("p j k -> p (j k)"), mb("hist")[:, 0:CTX * XB], ACT.Copy), "hist")
                act.drain().then_inc(prm_ready.sem, 1)
                yield due["small"]
                filled(act, l, "sm")
                sm = mb("sm").rearrange("p (t c) -> p t c", t=4)
                act.activation(TOKS[:, 0:2, 0:P], sm[:, 0:2, :], ACT.Copy)
                drained(act.activation(TOKS[0:DEC_SEQ, 2, 0:P], sm[0:DEC_SEQ, 2, :], ACT.Copy), "sm")
                act.drain().then_inc(toks.sem, 1)
                filled(act, l, "kic")
                act.activation(IKC[0:64, :], mb("kic")[0:64, 0:P], ACT.Copy)
                drained(act.activation(IKC[64:128, :], mb("kic")[0:64, 0:P], ACT.Copy), "kic")
                act.drain().then_inc(ikc.sem, 1)
                for h in range(IDX_HEADS):
                    yield due["ip", h]
                    if h >= 2:
                        act.wait_ge(idx_sum.sem, idx_sum.at(l, (h - 2) + 2 * ((h - 2) // 4) + 1))
                    filled(act, l, ("ip", h))
                    drained(act.activation(RP[:, h % 2, :], mb(("ip", h))[:, 0:384], ACT.Relu), ("ip", h))
                    act.drain().then_inc(relu_idx.sem, 1)
                    if h % 4 == 3:
                        if h >= 7:
                            act.wait_ge(idx_sum.sem, idx_sum.at(l, 6 * (h // 4)))
                        for odd in range(2):
                            key = ("is", h // 2 - 1 + odd)
                            filled(act, l, key)
                            drained(act.activation(RS[0:DEC_SEQ, odd, :], mb(key)[0:DEC_SEQ, 0:384], ACT.Relu), key)
                            act.drain().then_inc(relu_idx.sem, 1)
                for i, X_ in enumerate("ab"):
                    Q, PB, PT, STG = (mixer[X_][m] for m in (0, 5, 6, 7))
                    yield due[X_, "kct"]
                    key = (X_, "kct")
                    filled(act, l, key)
                    drained(act.activation(KCT, mb(key), ACT.Copy), key)
                    act.drain().then_inc(kct_ready.sem, 1)
                    for t, (o, n) in enumerate(TILES):
                        yield due[X_, "tok", t]
                        for w, (what, to) in enumerate((("ktok", STG[t % 2][0:n]), ("vtok", VTOK[0:n, t, :]))):
                            key = (X_, what, t)
                            if w == 0 and (i or t == 2):
                                act.wait_ge(rows_out[t % 2].sem, rows_out[t % 2].at(l, 2 * i + t // 2 if t != 1 else i))
                            if w == 1 and i and t == 0:
                                act.wait_ge(v_out.sem, v_out.at(l, 3))
                            filled(act, l, key)
                            drained(act.activation(to, mb(key)[0:n, :], ACT.Copy), key)
                            act.drain().then_inc(tok_out.sem, 1)
                    for t in range(4):
                        if t < 3:
                            yield due[X_, "lg", t]
                            n, S = TILES[t][1], KEYS[t]
                            act.wait_ge(att_max.sem, att_max.at(l, 3 * i + t + 1))
                            for h in range(HEADS):
                                act.activation(PB[0:n, h, 0:S], PB[0:n, h, 0:S], ACT.Exp, bias=small[0:n, 32 + h:33 + h],
                                               scale=1.0, accum_out=small[0:n, 36 + h:37 + h])
                            act.drain().then_inc(att_exp.sem, 1)
                        if t > 0:
                            yield due[X_, "pv", t - 1]
                            o, n = TILES[t - 1]
                            key = (X_, "pv", t - 1)
                            filled(act, l, key)
                            drained(act.activation(Q[:, :, o:o + n], mb(key)[:, 0:4 * n].rearrange("p (h t) -> p h t", h=4),
                                                   ACT.Copy), key)
                            act.drain().then_inc(att_out.sem, 1)
                        if t == 3:
                            continue
                        yield due[X_, "pt", t]
                        n = TILES[t][1]
                        for kt in range(2 if t == 1 else 1):
                            key = (X_, "pt", t, kt)
                            filled(act, l, key)
                            if t < 2:
                                drained(act.activation(PT[:, kt, :], mb(key), ACT.Copy), key)
                            else:
                                act.activation(PT[:, 0, 0:256], mb(key)[:, 0:256], ACT.Copy)
                                drained(act.activation(PT[0:n, 0, 256:512], mb(key)[0:n, 256:512], ACT.Copy), key)
                        act.drain().then_inc(att_pt.sem, 1)
                yield due["dt1"]
                act.activation(alog[:], alog[:], ACT.Exp)
                act.wait_ge(dt_exp.sem, dt_exp.at(l, 1))
                act.activation(tiny[:, 1, :, :], tiny[:, 1, :, :], ACT.Exp).then_inc(dt_u.sem, 1)
                yield due["dt2"]
                act.wait_ge(dt_ln.sem, dt_ln.at(l, 1))
                act.activation(tiny[:, 6, :, :], tiny[:, 3, :, :], ACT.Ln).then_inc(dt_done.sem, 1)
                yield due["dend"]
                act.wait_ge(dend_in.sem, dend_in.at(l, 1))
                act.activation(SDEC[:], SDEC[:], ACT.Exp)
                act.activation(DEND[:], DEND[:], ACT.Exp).then_inc(dend_ready.sem, 1)
                yield due["last"]
                filled(act, l, "last")
                drained(act.activation(lrow, mb("last")[0:2 * CTX * XB, 0:P], ACT.Copy), "last")
                act.drain().then_inc(lrow_ready.sem, 1)

                def decays(t, g):
                    k, n = 4 * t + g, TILES[t][1]
                    e_ = EX[0:n, k % 2, 0:HPG * n]
                    act.wait_ge(diff.sem, diff.at(l, k + 1))
                    if t:
                        drained(act.activation(EB[:, k % 2, 0:HPG * n], mb(("bc", t, g))[:, 0:HPG * n], ACT.Exp), ("bc", t, g))
                    act.activation(e_, e_, ACT.Exp).then_inc(ex_ready.sem, 1)

                def tile(t):
                    n = TILES[t][1]
                    filled(act, l, ("bt", t))
                    drained(act.activation(BT[0:n, :], mb(("bt", t))[0:n, :], ACT.Copy), ("bt", t))
                    act.drain().then_inc(bt_ready.sem, 1)

                def gate():
                    act.wait_ge(gz.sem, gz.at(l, 1))
                    for g in range(C_GROUPS):
                        act.activation(SQZ[:, 2 * g:2 * g + 2, :], Z[:, 2 * g:2 * g + 2, :], ACT.Square).then_inc(gsq.sem, 1)
                    for g in range(C_GROUPS):
                        key = ("gs", g)
                        filled(act, l, key)
                        drained(act.activation(GRMS[:, g, :], mb(key)[:, 0:TOK], ACT.Sqrt, scale=1.0 / (C_WIDTH // C_GROUPS),
                                               bias=eps[:, 0:1]), key)
                        act.drain().then_inc(grms.sem, 1)

                decays(0, 0)
                tile(0)
                for k, (t, g) in enumerate(groups):
                    yield due["y", t, g]
                    if k + 1 < len(groups):
                        decays(*groups[k + 1])
                    if g < C_GROUPS - 1:
                        continue
                    if t:
                        yield due["so", t]
                        if t == 2:
                            act.wait_ge(so_out.sem, so_out.at(l, 1))
                        for i in range(2):
                            key = ("so", t, i)
                            filled(act, l, key)
                            drained(act.activation(SO[:, i * UNIT:(i + 1) * UNIT], mb(key), ACT.Copy), key)
                        act.drain().then_inc(so_ready.sem, 1)
                    if t < 2:
                        yield due["tile", t + 1]
                        tile(t + 1)
                yield due["gate"]
                gate()

            def conv_newest_tap(half):
                act.wait_ge(conv_in.sem, conv_in.at(l, half + 1))
                xr = TB[:, :].rearrange("p (b t) -> p b t", b=BLKS)
                for b in range(BLKS):
                    kb = 4 * half + b
                    ins = act.activation(XC[:, kb, :], xr[:, b, CTX:CONVIN], ACT.Identity,
                                         scale=pcol("cw", CTX * XB + kb), bias=pcol("cb", kb))
                ins.then_inc(conv_tap.sem, 1)

            mix = Steps(mixers())
            for slot in range(2, SLOTS_AB + HALF):
                done, c = slot // CHUNKS - 1, slot % CHUNKS
                kind, _, half = PROJ[done] if 0 <= done < Q_OUT else ("", 0, 0)
                if slot + 1 < SLOTS_AB + HALF:
                    high_part(l, (slot + 1) // CHUNKS, (slot + 1) % CHUNKS)
                if slot == 7:
                    make_std(l, 0, "ssq0")
                if c == 1 and kind == "xbc":
                    conv_newest_tap(half)
                if c == 2 and kind == "z":
                    act.wait_ge(z_new.sem, z_new.at(l, half + 1))
                    z4 = Z[:, 4 * half:4 * half + 4, :]
                    act.activation(z4, z4, ACT.Silu).then_inc(z_ready.sem, 1)
                if c == 5 and kind == "xbc":
                    act.wait_ge(conv_out.sem, conv_out.at(l, half + 1))
                    x4 = XC[:, 4 * half:4 * half + 4, :]
                    act.activation(x4, x4, ACT.Silu).then_inc(xc_ready.sem, 1)
                mix.take(slot - LAG)
            mix.take(SLOTS_AB + CHUNKS * N_OUT)

            act.wait_ge(so_out.sem, so_out.at(l, 2))
            for stored in rows_out + [v_out]:
                act.wait_ge(stored.sem, stored.at(l, stored.per))
            for j in range(N_OUT):
                start = SLOTS_AB + HALF * j
                for slot in range(max(start + 3, SLOTS_AB + HALF), start + HALF + 3):
                    high_part(l, slot // CHUNKS, slot % CHUNKS)
                act.wait_ge(res_new.sem, res_new.at(l, j + 1))
                weigh(j, "mid")
                act.wait_ge(ss_done.sem, ss_done.at(l, j))
                square(j)

            def square_relu(f, j):
                for p_ in range(2):
                    act.wait_ge(relu_new.sem, relu_new.at(l, 8 * f + 2 * j + p_ + 1))
                    act.activation(U[:, 1, ds(4 * j + 2 * p_, 2), :],
                                   TB[:, 2 * p_ * TOK:(2 * p_ + 2) * TOK].rearrange("p (b t) -> p b t", b=2), ACT.Square)\
                        .then_inc(usq_new.sem, 1)

            high_parts(l, Q_MLP, 3, CHUNKS + 1)
            make_std(l, 1, "ssq1")
            high_parts(l, Q_MLP, CHUNKS + 1, CHUNKS + 3)
            square_relu(0, 0)
            with act.Fori(1, N_UP) as j:
                high_parts(l, Q_MLP + j, 3, CHUNKS + 3)
                square_relu(0, j)
            with act.Fori(1, QUARTERS) as f:
                with act.Fori(0, N_UP) as j:
                    high_parts(l, Q_MLP + 2 * N_UP * f - N_UP + j, 3, CHUNKS + 3)
                with act.Fori(0, N_UP) as j:
                    high_parts(l, Q_MLP + 2 * N_UP * f + j, 3, CHUNKS + 3)
                    square_relu(f, j)
            for j in range(N_UP):
                high_parts(l, UNITS - N_UP + j, 3, CHUNKS + 3 if j < N_UP - 1 else CHUNKS)
                if j < 3:
                    act.wait_ge(res_new.sem, res_new.at(l, 4 + j + 1))
                    weigh(j, "next")
                    act.wait_ge(ss_done.sem, ss_done.at(l, 4 + j))
                    square(j)
            act.drain().then_inc(layer_a.sem, 1)
        act.wait_ge(res_new.sem, res_new.at(DEPTH, 0))
        weigh(3, "next")
        act.wait_ge(ss_done.sem, ss_done.at(DEPTH, -1))
        square(3)

        k = 0
        for i in range(4):
            for t, (o, n) in enumerate(TILES):
                if k == 0:
                    act.wait_ge(fin_ss, 1)
                    for t_, (_, n_) in enumerate(TILES):
                        ins = act.activation(small[0:n_, t_:t_ + 1], M[0:n_, 3, t_:t_ + 1], ACT.Sqrt, scale=1.0 / D_MODEL,
                                             bias=eps[0:n_, 0:1])
                    ins.then_inc(fin_std, 1)
                    act.wait_ge(fin_rstd, 1)
                act.wait_ge(fin_full, k + 1)
                act.activation(Uf[0:n, k * UNIT:(k + 1) * UNIT], M[0:n, k % 3, :], ACT.Copy,
                               scale=small[0:n, 4 + t:5 + t]).then_inc(fin_row, 1)
                k += 1

    @block.vector
    def _(dve):
        def split_chunk(l, q, c):
            dve.wait_ge(high_done.sem, high_done.at(l, CHUNKS * q + c + 1))
            cols = slice(0, SMALL if isinstance(q, int) and q == Q_SMALL else UNIT)
            dve.tensor_tensor(wlo[:, c, :, cols], raw[:, c, :, cols], whi[:, c % 4, :, cols].bitcast(F32), ALU.subtract)\
                .then_inc(split_done.sem, 1)

        def chunks(l, q, first, last):
            for c in range(first, last):
                split_chunk(l, q, c)

        def next_unit(l, q):
            chunks(l, q + 1, 0, 2)

        def wait_low(l, reads):
            dve.wait_ge(low_pair_done.sem, low_pair_done.at(l, reads + 1 if isinstance(reads, int) and reads < Q_SMALL else reads))

        def wait_high(l, end):
            dve.wait_ge(chunk_used.sem, chunk_used.at(l, end))

        def pair(p):
            return G[:, 2 * p:2 * p + 2, 0:TOK]

        def rb(n=2):
            return rstd[:, :].unsqueeze(1).broadcast_to([P, n, TOK])

        def split_operand(full, parts, tiles):
            dve.tensor_copy(parts[:, 0, tiles, :], full[:, 1, tiles, :])
            dve.drain()
            return dve.tensor_tensor(parts[:, 1, tiles, :], full[:, 1, tiles, :],
                                     parts[:, 0, tiles, :].bitcast(F32), ALU.subtract)

        def make_rstd(l, k):
            dve.wait_ge(std_done.sem, std_done.at(l, k + 1))
            dve.reciprocal(rstd[:], STD[:])
            dve.drain()

        dve.sem_inc(low_free.sem, 1)
        dve.sem_inc(high_free.sem, 1)
        dve.sem_inc(res_new.sem, 1)
        for b in range(4):
            dve.sem_inc(banks.drained[b].sem, 1)
        for j in range(3):
            dve.wait_ge(weighed.sem, j + 1)
            split_operand(X, X_parts, slice(4 * j, 4 * j + 4)).then_inc(x_in.sem, 1)
        dve.sem_inc(layer_v.sem, 1)

        def rope_swapped(x, tab, rows, n):
            shift = 16 if tab is ropeA else 8
            mask = [(i + shift) % (2 * shift) if i < 2 * shift else i for i in range(32)]
            sin = tab[rows, 1, :].unsqueeze(1).broadcast_to([x.shape[0], n, TOK])
            t = TB[rows, 0:n * TOK].rearrange("p (b t) -> p b t", b=n)
            dve.stream_shuffle(t, x, mask)
            dve.drain()
            dve.tensor_tensor(t, t, sin, ALU.mult)
            dve.drain()

        def rope_sum(x, tab, rows, n):
            cos = tab[rows, 0, :].unsqueeze(1).broadcast_to([x.shape[0], n, TOK])
            dve.tensor_tensor(x, x, cos, ALU.mult)
            dve.drain()
            dve.tensor_tensor(x, x, TB[rows, 0:n * TOK].rearrange("p (b t) -> p b t", b=n), ALU.add)

        with dve.Fori(0, DEPTH) as l:
            def place(kind, half):
                return {"iq": IQ[:, 4 * half:4 * half + 4, :], "ak": AK, "aq": AQ, "av": AV, "bq": BQ, "bk": BK,
                        "bv": BV, "z": Z[:, 4 * half:4 * half + 4, :]}[kind]

            def conv_rows():
                return TB[:, :].rearrange("p (b t) -> p b t", b=BLKS)

            def read_out(q):
                kind, _, half = PROJ[q]
                end = CHUNKS * (q + 1)
                if q == 0:
                    make_rstd(l, 0)
                if kind == "small":
                    wait_high(l, end)
                    dve.tensor_tensor(SM, G[:, 0, 0:TOK], rstd[:], ALU.mult).then_inc(low_free.sem, 1)
                    dve.drain()
                    rope_swapped(SM[0:32, :].unsqueeze(1), ropeI, slice(0, 32), 1)
                    rope_sum(SM[0:32, :].unsqueeze(1), ropeI, slice(0, 32), 1)
                    dve.drain()
                    dve.tensor_copy(IKD[64:128, :], SM[0:64, :]).then_inc(ikd.sem, 1)
                    dve.drain().then_inc(proj_out.sem, 1)
                elif kind != "xbc":
                    dst = place(kind, half)
                    wait_low(l, q)
                    dve.tensor_tensor(dst[:, 0:2, :], pair(0), rb(), ALU.mult).then_inc(low_free.sem, 1)
                    wait_high(l, end)
                    dve.tensor_tensor(dst[:, 2:4, :], pair(1), rb(), ALU.mult).then_inc(high_free.sem, 1)
                    dve.drain()
                    if kind in ("av", "bq", "bk", "bv"):
                        dve.drain().then_inc(proj_out.sem, 1)
                    if kind == "z":
                        dve.drain().then_inc(z_new.sem, 1)
                else:
                    xr = conv_rows()
                    dve.memset(xr[:, :, 0:CTX], 0.0)
                    if half == 0:
                        dve.wait_ge(prm_ready.sem, prm_ready.at(l, 2))
                    f4 = slice(4 * half, 4 * half + 4)
                    dve.tensor_copy(xr[:, :, CTX + SEQ:2 * CTX + SEQ], HIST[:, :, f4].rearrange("p j k -> p k j"))
                    for p_ in range(2):
                        if p_ == 0:
                            wait_low(l, q)
                        else:
                            wait_high(l, end)
                        b2 = slice(2 * p_, 2 * p_ + 2)
                        dve.tensor_tensor(xr[:, b2, CTX:CTX + SEQ], pair(p_)[:, :, 0:SEQ],
                                          rstd[:, 0:SEQ].unsqueeze(1).broadcast_to([P, 2, SEQ]), ALU.mult)
                        dve.tensor_tensor(xr[:, b2, 2 * CTX + SEQ:], pair(p_)[:, :, SEQ:TOK],
                                          rstd[:, SEQ:TOK].unsqueeze(1).broadcast_to([P, 2, DEC_SEQ]), ALU.mult)\
                            .then_inc((low_free if p_ == 0 else high_free).sem, 1)
                    dve.drain().then_inc(conv_in.sem, 1)
                    dve.tensor_copy(LAST[:, 0, :, f4].rearrange("p r k -> p k r"), xr[:, :, SEQ:SEQ + CTX])
                    dve.tensor_copy(LAST[:, 1, :, f4].rearrange("p r k -> p k r"), xr[:, :, CONVIN - CTX:CONVIN])\
                        .then_inc(last_in.sem, 1)

            def finish(q, part):
                kind, _, half = PROJ[q]
                if kind in ("iq", "aq", "ak"):
                    dst = place(kind, half)
                    tab, rows = (ropeI, slice(0, P)) if kind == "iq" else (ropeA, slice(0, 32))
                    if part == 0:
                        rope_swapped(dst[rows], tab, rows, BLKS)
                    if part == 1:
                        rope_sum(dst[rows], tab, rows, BLKS)
                        if kind == "iq" and half == 0:
                            dve.drain()
                        else:
                            dve.drain().then_inc(proj_out.sem, 1)
                if kind == "xbc":
                    j, xr = part, conv_rows()
                    if part == 0:
                        dve.wait_ge(conv_tap.sem, conv_tap.at(l, half + 1))
                    for b in range(BLKS):
                        kb = BLKS * half + b
                        dve.scalar_tensor_tensor(out=XC[:, kb, :], in0=xr[:, b, j:j + CONVOUT],
                                                 scalar=pcol("cw", j * XB + kb), in1=XC[:, kb, :],
                                                 op0=ALU.mult, op1=ALU.add)
                    if part == CONV_W - 2:
                        dve.drain().then_inc(conv_out.sem, 1)
                    else:
                        dve.drain()

            def add_residual(reads, j, end):
                for p_ in range(2):
                    if p_ == 0:
                        wait_low(l, reads)
                    else:
                        wait_high(l, end)
                    x2 = xT[:, ds(4 * j + 2 * p_, 2), :]
                    dve.tensor_tensor(x2, x2, pair(p_), ALU.add).then_inc((low_free if p_ == 0 else high_free).sem, 1)
                dve.drain()

            def mix_operand(j):
                m4 = MIX[:, 4 * j:4 * j + 4, :]
                hi, lo = (U_parts[:, i, 4 * j:4 * j + 4, :] for i in range(2))
                dve.tensor_copy(hi, m4)
                dve.drain()
                return dve.tensor_tensor(lo, m4, hi.bitcast(F32), ALU.subtract)

            def mixers():
                yield due["ip", 0]
                dve.wait_ge(toks.sem, toks.at(l, 1))
                iw = tiny[:, 5, :, :]
                dve.tensor_scalar(iw, TOKS[:, :, R_IW:R_IW + IDX_HEADS], IW_SCALE, None, ALU.mult)
                dve.drain()
                for h in range(IDX_HEADS):
                    yield due["ip", h]
                    k = h + 2 * (h // 4)
                    dve.wait_ge(relu_idx.sem, relu_idx.at(l, k + 1))
                    r = RP[:, h % 2, :]
                    if h == 0:
                        dve.tensor_scalar(ABIAS, r[:, 0:SEQ], iw[:, 1, h:h + 1], None, ALU.mult)
                        dve.tensor_scalar(ABIAS0, r[:, SEQ:384], iw[:, 0, h:h + 1], None, ALU.mult).then_inc(idx_sum.sem, 1)
                    else:
                        dve.scalar_tensor_tensor(out=ABIAS, in0=r[:, 0:SEQ], scalar=iw[:, 1, h:h + 1], in1=ABIAS,
                                                 op0=ALU.mult, op1=ALU.add)
                        dve.scalar_tensor_tensor(out=ABIAS0, in0=r[:, SEQ:384], scalar=iw[:, 0, h:h + 1], in1=ABIAS0,
                                                 op0=ALU.mult, op1=ALU.add).then_inc(idx_sum.sem, 1)
                    dve.drain()
                    if h % 4 != 3:
                        continue
                    acc = ABIASS[0:DEC_SEQ]
                    for odd in range(2):
                        dve.wait_ge(relu_idx.sem, relu_idx.at(l, k + 2 + odd))
                        for i in range(2):
                            r = RS[0:DEC_SEQ, odd, 192 * i:192 * i + 192]
                            hh = h - 3 + odd + 2 * i
                            w = iw[0:DEC_SEQ, 2, hh:hh + 1]
                            if hh == 0:
                                ins = dve.tensor_scalar(acc, r, w, None, ALU.mult)
                            else:
                                ins = dve.scalar_tensor_tensor(out=acc, in0=r, scalar=w, in1=acc, op0=ALU.mult, op1=ALU.add)
                            if i == 0:
                                dve.drain()
                        ins.then_inc(idx_sum.sem, 1)
                        dve.drain()

                work = [(ABIAS0, seen[:, P:SEQ], TOPK_P), (ABIAS, seen[:, :], TOPK_P),
                        (ABIASS[0:DEC_SEQ], None, TOPK_S)]
                yield due["top", 0]
                for w, mask, _ in work[:2]:
                    dve.scalar_tensor_tensor(out=w, in0=mask, scalar=NOT_SEEN / NEG, in1=w, op0=ALU.mult, op1=ALU.add)
                dve.drain()
                for r in range(TOPK_P // 8):
                    yield due["top", r]
                    for i, (w, _, topk) in enumerate(work):
                        if 8 * r < topk:
                            dve.max(small[0:w.shape[0], 8 * i:8 * i + 8], w)
                    dve.drain()
                    for i, (w, _, topk) in enumerate(work):
                        if 8 * r < topk:
                            dve.match_replace(w, small[0:w.shape[0], 8 * i:8 * i + 8], w, TAKEN)
                    dve.drain()
                yield due["chosen"]
                for w, _, _ in work:
                    dve.tensor_scalar(w, w, TAKEN, NEG, ALU.not_equal, ALU.mult)
                dve.drain()

                for i, X_ in enumerate("ab"):
                    PB = mixer[X_][5]
                    if X_ == "b":
                        yield due["b", "kct"]
                        dve.wait_ge(cache_b_in.sem, cache_b_in.at(l, 3))
                        dve.tensor_tensor(BBIAS, BBIAS, seen[:, :].unsqueeze(1).broadcast_to([P, HEADS, SEQ]), ALU.add)
                        dve.drain()
                    for t, (o, n) in enumerate(TILES):
                        yield due[X_, "lg", t]
                        S = KEYS[t]
                        per = HEADS if t == 0 else 2
                        if t:
                            dve.wait_ge(att_pt.sem, att_pt.at(l, 3 * i + t))
                        for j in range(HEADS // per):
                            key = (X_, "lg", t, j)
                            filled(dve, l, key)
                            if X_ == "a":
                                bias = ((ABIAS0, ABIAS, ABIASS)[t][0:n]).unsqueeze(1).broadcast_to([n, per, S])
                            else:
                                at = P if t == 0 else 0
                                bias = BBIAS[0:n, j * per:(j + 1) * per, at:at + S]
                            drained(dve.scalar_tensor_tensor(
                                out=PB[0:n, j * per:(j + 1) * per, 0:S],
                                in0=mb(key)[0:n, 0:per * S].rearrange("p (h s) -> p h s", h=per),
                                scalar=SCALE, in1=bias, op0=ALU.mult, op1=ALU.add), key)
                        dve.drain()
                        dve.tensor_reduce(small[0:n, 32:36], PB[0:n, :, 0:S], AX_X, ALU.max, negate=True)\
                            .then_inc(att_max.sem, 1)
                        yield due[X_, "p", t]
                        dve.wait_ge(att_exp.sem, att_exp.at(l, 3 * i + t + 1))
                        dve.reciprocal(small[0:n, 40:44], small[0:n, 36:40])
                        dve.drain()
                        for h in range(HEADS):
                            ins = dve.tensor_scalar(PB[0:n, h, 0:S], PB[0:n, h, 0:S], small[0:n, 40 + h:41 + h], None, ALU.mult)
                        ins.then_inc(att_p.sem, 1)

                yield due["ab"]
                dve.wait_ge(att_out.sem, att_out.at(l, 6))
                for stored in rows_out + [v_out]:
                    dve.wait_ge(stored.sem, stored.at(l, stored.per))
                for j in range(2):
                    mix_operand(j).then_inc(x_mix.sem, 1)

                yield due["dt1"]
                v, e, c, u, lg = DT[:, :, :], tiny[:, 1, :, :], tiny[:, 2, :, :], tiny[:, 3, :, :], tiny[:, 4, :, :]
                dve.tensor_tensor(v, TOKS[:, :, R_DT:R_DT + C_HEADS], dtb[:, :].unsqueeze(1).broadcast_to([P, 3, C_HEADS]), ALU.add)
                dve.drain()
                dve.scalar_tensor_tensor(out=e, in0=v, scalar=-1.0, in1=v, op0=ALU.mult, op1=ALU.min).then_inc(dt_exp.sem, 1)
                yield due["dt2"]
                dve.wait_ge(dt_u.sem, dt_u.at(l, 1))
                dve.tensor_scalar(u, e, 1.0, None, ALU.add).then_inc(dt_ln.sem, 1)
                dve.drain()
                dve.tensor_scalar(c, u, -1.0, None, ALU.add)
                dve.reciprocal(lg, u)
                dve.drain()
                dve.tensor_tensor(c, e, c, ALU.subtract)
                dve.drain()
                dve.tensor_tensor(c, c, lg, ALU.mult)
                dve.tensor_scalar(v, v, 0.0, None, ALU.max)
                dve.drain()
                dve.tensor_tensor(v, v, c, ALU.add)
                dve.drain()
                yield due["ad"]
                dve.wait_ge(dt_done.sem, dt_done.at(l, 1))
                dve.tensor_tensor(v, v, tiny[:, 6, :, :], ALU.add)
                dve.drain()
                dve.scalar_tensor_tensor(out=tiny[:, 0, :, :], in0=v, scalar=-1.0,
                                         in1=alog[:, :].unsqueeze(1).broadcast_to([P, 3, C_HEADS]),
                                         op0=ALU.mult, op1=ALU.mult).then_inc(ad_ready.sem, 1)
                yield due["acs"]
                filled(dve, l, "acs")
                for t, (o, n) in enumerate(TILES):
                    dve.tensor_copy(ACS[0:n, t, :], mb("acs")[0:n, t * C_HEADS:(t + 1) * C_HEADS])
                dve.drain().then_inc(acs_ready.sem, 1)
                dve.tensor_scalar(NACS[:], ACS[:], -1.0, None, ALU.mult)
                drained(dve.drain(), "acs")
                yield due["acst"]
                filled(dve, l, "acst")
                drained(dve.tensor_copy(ACST[:, :], mb("acst")[0:C_HEADS, 0:TOK]), "acst")
                dve.drain().then_inc(acst_ready.sem, 1)
                yield due["aend"]
                filled(dve, l, "aend")
                dve.tensor_copy(SDEC[:], mb("aend")[:, 0:3 * C_HEADS].rearrange("p (t h) -> p t h", t=3))
                drained(dve.tensor_tensor(DEND[:], mb("aend")[:, 0:3 * C_HEADS].rearrange("p (t h) -> p t h", t=3), ACS[:],
                                          ALU.subtract), "aend")
                dve.drain().then_inc(dend_in.sem, 1)
                def log_decays(t, g):
                    k, n = 4 * t + g, TILES[t][1]
                    e_ = EX[0:n, k % 2, 0:HPG * n]
                    filled(dve, l, ("bc", t, g))
                    for j in range(HPG):
                        h = HPG * g + j
                        ins = dve.scalar_tensor_tensor(out=e_[:, j * n:(j + 1) * n],
                                                       in0=mb(("bc", t, g))[0:n, j * n:(j + 1) * n],
                                                       scalar=NACS[0:n, t, h:h + 1], in1=tri[0:n, 0, 0:n],
                                                       op0=ALU.add, op1=ALU.min)
                    ins.then_inc(diff.sem, 1)
                    if t == 0:
                        drained(dve.drain(), ("bc", t, g))

                def weights(t, g):
                    k, at, n = 4 * t + g, CONV_AT[t], TILES[t][1]
                    e_, m_ = EX[0:n, k % 2, 0:HPG * n], MM[0:n, k % 2, 0:HPG * n]
                    eb, ct = EB[:, k % 2, 0:HPG * n], CTS[:, k % 2, 0:HPG * n]
                    dve.wait_ge(ex_ready.sem, ex_ready.at(l, k + 1))
                    key = ("cb", t, g)
                    filled(dve, l, key)
                    ins = dve.tensor_tensor(m_.rearrange("p (j s) -> p j s", j=HPG), e_.rearrange("p (j s) -> p j s", j=HPG),
                                            mb(key)[0:n, 0:n].unsqueeze(1).broadcast_to([n, HPG, n]), ALU.mult)
                    drained(ins, key)
                    dve.drain().then_inc(mm_ready.sem, 1)
                    if t:
                        dve.tensor_tensor(ct.rearrange("p (j s) -> p j s", j=HPG), eb.rearrange("p (j s) -> p j s", j=HPG),
                                          XC[:, 12 + g, at:at + n].unsqueeze(1).broadcast_to([P, HPG, n]), ALU.mult)\
                            .then_inc(cts_ready.sem, 1)
                    else:
                        dve.drain().then_inc(cts_ready.sem, 1)

                def tile(t):
                    n = TILES[t][1]
                    if t == 2:
                        dve.wait_ge(so_ready.sem, so_ready.at(l, 1))
                        for i in range(2):
                            key = ("si", i)
                            filled(dve, l, key)
                            drained(dve.tensor_copy(ST[:, i * UNIT:(i + 1) * UNIT], mb(key)), key)
                        dve.drain().then_inc(st_first.sem, 1)
                    hb = [n, 8, C_HD]
                    for i in range(2):
                        key = ("xt", t, i)
                        filled(dve, l, key)
                        drained(dve.tensor_tensor(XD[0:n, i * UNIT:(i + 1) * UNIT].rearrange("p (h d) -> p h d", d=C_HD),
                                                  mb(key)[0:n, :].rearrange("p (h d) -> p h d", d=C_HD),
                                                  DT[0:n, t, 8 * i:8 * i + 8].unsqueeze(2).broadcast_to(hb), ALU.mult), key)
                    dve.drain()
                    if t == 0:
                        dve.wait_ge(dend_ready.sem, dend_ready.at(l, 1))
                    dve.tensor_tensor(XDD[0:n, :].rearrange("p (h d) -> p h d", d=C_HD),
                                      XD[0:n, :].rearrange("p (h d) -> p h d", d=C_HD),
                                      DEND[0:n, t, :].unsqueeze(2).broadcast_to([n, C_HEADS, C_HD]), ALU.mult)\
                        .then_inc(xd_ready.sem, 1)

                def gated(t, g):
                    k, at = 4 * t + g, CONV_AT[t]
                    o, n = TILES[t]
                    key = ("y", t, g)
                    filled(dve, l, key)
                    for p in range(2):
                        kb = 2 * g + p
                        for half in range(2):
                            r = slice(64 * half, 64 * half + 64)
                            ins = dve.scalar_tensor_tensor(
                                out=YT[r, p, 0:n], in0=XC[r, kb, at:at + n], scalar=dskip[r, kb:kb + 1],
                                in1=mb(key)[r, (2 * p + half) * n:(2 * p + half + 1) * n], op0=ALU.mult, op1=ALU.add)
                    drained(ins, key)
                    dve.drain()
                    if k == 0:
                        dve.wait_ge(z_ready.sem, z_ready.at(l, 2))
                    dve.tensor_tensor(Z[:, 2 * g:2 * g + 2, o:o + n], Z[:, 2 * g:2 * g + 2, o:o + n], YT[:, :, 0:n], ALU.mult)
                    key = ("st", t, g)
                    filled(dve, l, key)
                    s_ = ST[:, g * 256:(g + 1) * 256]
                    if t == 0:
                        drained(dve.tensor_copy(s_, mb(key)[:, 0:256]), key)
                    else:
                        dve.tensor_tensor(s_.rearrange("p (h d) -> p h d", d=C_HD), s_.rearrange("p (h d) -> p h d", d=C_HD),
                                          SDEC[:, t, HPG * g:HPG * g + HPG].unsqueeze(2).broadcast_to([P, HPG, C_HD]), ALU.mult)
                        dve.drain()
                        drained(dve.tensor_tensor(s_, s_, mb(key)[:, 0:256], ALU.add), key)
                    dve.drain().then_inc(st_ready.sem, 1)

                def gate():
                    for g in range(C_GROUPS):
                        dve.wait_ge(grms.sem, grms.at(l, g + 1))
                        dve.reciprocal(GRMS[:, g, :], GRMS[:, g, :])
                        dve.drain()
                        for b in range(2):
                            zb = Z[:, 2 * g + b, :]
                            dve.scalar_tensor_tensor(out=zb, in0=zb, scalar=pcol("gate", 2 * g + b), in1=GRMS[:, g, :],
                                                     op0=ALU.mult, op1=ALU.mult)
                        if g % 2:
                            dve.drain()
                            mix_operand(2 + g // 2).then_inc(x_mix.sem, 1)

                yield due["cb"]
                log_decays(0, 0)
                weights(0, 0)
                tile(0)
                for k, (t, g) in enumerate(groups):
                    yield due["y", t, g]
                    if k + 1 < len(groups):
                        log_decays(*groups[k + 1])
                    gated(t, g)
                    if k + 1 < len(groups):
                        weights(*groups[k + 1])
                    if g == C_GROUPS - 1 and t < 2:
                        yield due["tile", t + 1]
                        tile(t + 1)
                dve.drain().then_inc(gz.sem, 1)
                yield due["gate"]
                gate()

            mix = Steps(mixers())
            for slot in range(SLOTS_AB + HALF):
                q, c = slot // CHUNKS, slot % CHUNKS
                split_chunk(l, q, c)
                if slot == 1:
                    dve.wait_ge(weighed.sem, weighed.at(l, 0))
                    split_operand(X, X_parts, slice(12, 16)).then_inc(x_in.sem, 1)
                if q == 1 and c == 0:
                    dve.wait_ge(consts_in, 16 * 4)
                    dve.wait_ge(ones_set, 4)
                if c == 1 and 0 < q <= Q_OUT:
                    read_out(q - 1)
                    if q == Q_OUT:
                        dve.sem_inc(x_free.sem, 1)
                if 0 < q <= Q_OUT and 2 <= c < 5:
                    finish(q - 1, c - 2)
                if slot % HALF == 1 and slot > SLOTS_PROJ + HALF:
                    j = (slot - SLOTS_PROJ) // HALF - 1
                    add_residual(Q_OUT + j, j, slot - 1)
                mix.take(slot - LAG)
            mix.take(SLOTS_AB + CHUNKS * N_OUT)

            def new_operand(l, j, k, ready):
                dve.drain().then_inc(res_new.sem, 1)
                if k < 7:
                    dve.wait_ge(weighed.sem, weighed.at(l, k + 1))
                    split_operand(X, X_parts, slice(4 * j, 4 * j + 4)).then_inc(ready.sem, 1)

            for j in range(N_OUT):
                start = SLOTS_AB + HALF * j
                for slot in range(max(start + 2, SLOTS_AB + HALF), start + HALF + 2):
                    split_chunk(l, slot // CHUNKS, slot % CHUNKS)
                add_residual(Q_OUT + N_OUT + j, j, start + HALF)
                new_operand(l, j, j, x_mid)

            def relu_half(l, q, p_):
                t2 = TB[:, 2 * p_ * TOK:(2 * p_ + 2) * TOK].rearrange("p (b t) -> p b t", b=2)
                if p_ == 0:
                    wait_low(l, q + MORE)
                else:
                    wait_high(l, CHUNKS * (q + 1))
                ins = dve.scalar_tensor_tensor(out=t2, in0=pair(p_), scalar=0.0, in1=rb(), op0=ALU.max, op1=ALU.mult)
                ins.then_inc((low_free if p_ == 0 else high_free).sem, 1)
                dve.drain().then_inc(relu_new.sem, 1)

            def up_unit(l, q, f, j):
                relu_half(l, q, 0)
                relu_half(l, q, 1)
                for p_ in range(2):
                    dve.wait_ge(usq_new.sem, usq_new.at(l, 8 * f + 2 * j + p_ + 1))
                    ins = split_operand(U, U_parts, ds(4 * j + 2 * p_, 2))
                ins.then_inc(u_ready.sem, 1)

            chunks(l, Q_MLP, 2, CHUNKS)
            next_unit(l, Q_MLP)
            make_rstd(l, 1)
            up_unit(l, Q_MLP, 0, 0)
            with dve.Fori(1, N_UP) as j:
                q = Q_MLP + j
                chunks(l, q, 2, CHUNKS)
                next_unit(l, q)
                up_unit(l, q, 0, j)
            with dve.Fori(1, QUARTERS) as f:
                with dve.Fori(0, N_UP) as j:
                    q = Q_MLP + 2 * N_UP * f - N_UP + j
                    chunks(l, q, 2, CHUNKS)
                    next_unit(l, q)
                    add_residual(q + MORE, j, CHUNKS * (q + 1))
                with dve.Fori(0, N_UP) as j:
                    q = Q_MLP + 2 * N_UP * f + j
                    chunks(l, q, 2, CHUNKS)
                    next_unit(l, q)
                    up_unit(l, q, f, j)
            for j in range(N_UP):
                q = UNITS - N_UP + j
                chunks(l, q, 2, CHUNKS)
                if j < N_UP - 1:
                    next_unit(l, q)
                add_residual(q + MORE, j, CHUNKS * (q + 1))
                new_operand(l, j, 4 + j, x_in)
            dve.drain().then_inc(layer_v.sem, 1)

        for j in range(4):
            dve.wait_ge(sq_done.sem, sq_done.at(DEPTH, j - 3))
            x4 = xT[:, 4 * j:4 * j + 4, :]
            if j < 3:
                ins = dve.tensor_tensor(x4, X_parts[:, 0, 4 * j:4 * j + 4, :].bitcast(F32),
                                        X_parts[:, 1, 4 * j:4 * j + 4, :].bitcast(F32), ALU.add)
            else:
                ins = dve.tensor_copy(x4, X[:, 1, 4 * j:4 * j + 4, :])
            ins.then_inc(fin_new, 1)
        dve.wait_ge(fin_std, 1)
        for t, (_, n) in enumerate(TILES):
            ins = dve.reciprocal(small[0:n, 4 + t:5 + t], small[0:n, t:t + 1])
        ins.then_inc(fin_rstd, 1)

    block.__exit__(None, None, None)


def constants():
    f = np.float32
    q, k = np.arange(P)[:, None], np.arange(SEQ)[None]
    seen = np.where(k < P + 64 * (q // 64 + 1), 0, NEG).astype(f)
    s, t = np.arange(P)[:, None], np.arange(P)[None]
    tri = np.stack([np.where(s <= t, 0, NEG), (s <= t)], axis=1).astype(f)
    pos = np.concatenate([np.arange(SEQ), PAST + np.arange(DEC_SEQ)]).astype(f)
    rope = np.zeros((2, P, 2, TOK), f)
    rope[:, :, 0] = 1
    for i, (dim, starts) in enumerate(((HD, (0,)), (IDX_DIM, (0, 64)))):
        rot = dim // 4
        half = rot // 2
        inv = f(500000.0) ** (-np.arange(half, dtype=f) * f(2.0) / f(rot))
        ang = (pos[None, :] * inv[:, None]).astype(f)
        for a in starts:
            for j in (0, half):
                rope[i, a + j:a + j + half, 0] = np.cos(ang)
            rope[i, a:a + half, 1] = -np.sin(ang)
            rope[i, a + half:a + rot, 1] = np.sin(ang)
    return {"ident": np.eye(P, dtype=f), "seen": seen, "tri": tri, "rope": rope}


def kernel(x_prompt, x_sample, cache_a_k, cache_a_v, cache_a_kidx, cache_b_k, cache_b_v, state_ssm, state_conv,
           norm1, w_in, w_out, b_rel, conv_w, conv_b, dt_bias, a_log, d_skip, gate_norm, norm2, w_up, w_down,
           final_norm):
    import concourse.bacc as bacc
    from concourse.bass_utils import run_bass_kernel_spmd

    a = np.ascontiguousarray
    n1, n2, nf = (np.asarray(v) for v in (norm1, norm2, final_norm))
    norms = np.concatenate([v for i in range(DEPTH) for v in (n1[i:i + 1], n2[i:i + 1])] + [nf[None]])
    skip = np.repeat(np.asarray(d_skip), C_HD, axis=1).reshape(DEPTH, C_WIDTH // P, P).transpose(0, 2, 1)
    c = constants()
    ins = dict(x_prompt=x_prompt, x_sample=x_sample, cache_a_k=cache_a_k, cache_a_v=cache_a_v,
               cache_a_kidx=cache_a_kidx, cache_b_k=cache_b_k, cache_b_v=cache_b_v, state_ssm=state_ssm,
               state_conv=state_conv, norms=norms, w_in=w_in, w_out=w_out, b_rel_rev=np.asarray(b_rel)[:, :, ::-1],
               conv_w=conv_w, conv_b=conv_b, dt_bias=dt_bias, a_log=a_log, d_skip=skip, gate_norm=gate_norm,
               w_up=w_up, w_down=w_down, ident=c["ident"], seen=c["seen"], tri=c["tri"], rope=c["rope"])
    kv = (HEADS, HD)
    outs = dict(y_prompt=(1, SEQ, D_MODEL), y_sample=(1, DEC_SEQ, D_MODEL),
                p_a_k=(DEPTH, 1, SEQ) + kv, p_a_v=(DEPTH, 1, SEQ) + kv, p_a_kidx=(DEPTH, 1, SEQ, IDX_DIM),
                p_b_k=(DEPTH, 1, SEQ) + kv, p_b_v=(DEPTH, 1, SEQ) + kv,
                p_ssm=(DEPTH, 1, C_HEADS, C_HD, C_STATE), p_conv=(DEPTH, 1, CTX, CONV_DIM),
                s_a_k=(DEPTH, 1, DEC_SEQ) + kv, s_a_v=(DEPTH, 1, DEC_SEQ) + kv, s_a_kidx=(DEPTH, 1, DEC_SEQ, IDX_DIM),
                s_b_k=(DEPTH, 1, DEC_SEQ) + kv, s_b_v=(DEPTH, 1, DEC_SEQ) + kv,
                s_ssm=(DEPTH, 1, C_HEADS, C_HD, C_STATE), s_conv=(DEPTH, 1, CTX, CONV_DIM))
    nc = bacc.Bacc("TRN2", target_bir_lowering=False, num_devices=1, dynamic_dma_scratch_size=8192)
    arrays, args = {}, []
    for name, v in ins.items():
        arrays["in_" + name] = a(v)
        args.append(nc.dram_tensor("in_" + name, arrays["in_" + name].shape, F32, kind="ExternalInput").ap())
    for name, shape in outs.items():
        args.append(nc.dram_tensor("out_" + name, shape, F32, kind="ExternalOutput").ap())
    trunk(nc, *args)
    r = run_bass_kernel_spmd(nc, [arrays], core_ids=[0])
    return tuple(r.results[0]["out_" + name] for name in outs)
```
